# Optimizing a Trainium2 kernel written in Bass

```python
import math
import jax, jax.numpy as jnp
from jax import lax
import numpy as np

D_MODEL = 2048
BATCH = 1
SEQ = 256
DEPTH = 2
DEC_BATCH = 8
DEC_SEQ = 4
PAST_LEN = 2048
PAGE_SIZE = 128

HEAD_DIM = 128
H_A = 4
H_B = 4
H_C = 8
D_A = H_A * HEAD_DIM
D_B = H_B * HEAD_DIM
D_C = H_C * HEAD_DIM
D_MIX = D_A + D_B + D_C
D_FF = 4 * D_MODEL
CONV_W = 4
CHUNK = 64
ROPE_BASE = 10000.0
GATE_SOFTCAP = 15.0
NORM_EPS = 1e-6
IN_SPLITS = (D_A, D_A, D_A, D_A, H_A, H_A, D_B, D_B, D_B, D_B, D_C, D_C, D_C, D_C, H_C, H_C)
N_IN = 4 * D_A + 2 * H_A + 4 * D_B + 4 * D_C + 2 * H_C

kernel_name = 'hybrid_mlstm_retention_gdn_decoder_step'

def _rmsnorm(x, g):
    xf = x.astype(jnp.float32)
    xf = xf * lax.rsqrt(jnp.mean(xf * xf, axis=-1, keepdims=True) + NORM_EPS)
    return (xf * g.astype(jnp.float32)).astype(x.dtype)

def _head_norm(x, g, center):
    if center:
        x = x - jnp.mean(x, axis=-1, keepdims=True)
    x = x * lax.rsqrt(jnp.mean(x * x, axis=-1, keepdims=True) + NORM_EPS)
    x = x * g.astype(jnp.float32).reshape(-1, x.shape[-1])
    return x.reshape(x.shape[:2] + (-1,))

def _l2norm(x):
    return x * lax.rsqrt(jnp.sum(x * x, axis=-1, keepdims=True) + NORM_EPS)

def _rotary(x, pos):
    half = x.shape[-1] // 2
    inv = ROPE_BASE ** (-jnp.arange(half, dtype=jnp.float32) / half)
    ang = pos.astype(jnp.float32)[:, None] * inv[None, :]
    cos = jnp.cos(ang)[None, :, None, :]
    sin = jnp.sin(ang)[None, :, None, :]
    x1, x2 = x[..., :half], x[..., half:]
    return jnp.concatenate([x1 * cos - x2 * sin, x1 * sin + x2 * cos], axis=-1)

def _to_chunks(x, L):
    B, T = x.shape[:2]
    x = x.reshape((B, T // L, L) + x.shape[2:])
    return jnp.moveaxis(jnp.moveaxis(x, 1, 0), 2, 3)

def _from_chunks(y):
    y = jnp.moveaxis(jnp.moveaxis(y, 0, 1), 2, 3)
    B, nC, L = y.shape[:3]
    return y.reshape((B, nC * L) + y.shape[3:])

def _mlstm(q, k, v, ig, lf, C0, n0, m0):
    L = math.gcd(q.shape[1], CHUNK)
    incl = jnp.tril(jnp.ones((L, L), dtype=bool))

    def chunk(carry, xs):
        C, n, mp = carry
        qc, kc, vc, ic, fc = xs
        F = jnp.cumsum(fc, axis=-1)
        m = F + jnp.maximum(mp[..., None], lax.cummax(ic - F, axis=2))
        logw = F[..., :, None] - F[..., None, :] + ic[..., None, :] - m[..., :, None]
        s = jnp.einsum('bhid,bhjd->bhij', qc, kc) * jnp.exp(jnp.where(incl, logw, -jnp.inf))
        inter = jnp.exp(F + mp[..., None] - m)
        num = inter[..., None] * jnp.einsum('bhid,bhde->bhie', qc, C) + jnp.einsum('bhij,bhje->bhie', s, vc)
        den = inter * jnp.einsum('bhid,bhd->bhi', qc, n) + jnp.sum(s, axis=-1)
        h = num / jnp.maximum(jnp.abs(den), jnp.exp(-m))[..., None]
        m_new = m[..., -1]
        wl = jnp.exp(ic + F[..., -1:] - F - m_new[..., None])
        dec = jnp.exp(F[..., -1] + mp - m_new)
        kw = kc * wl[..., None]
        C = dec[..., None, None] * C + jnp.einsum('bhjd,bhje->bhde', kw, vc)
        n = dec[..., None] * n + jnp.sum(kw, axis=2)
        return (C, n, m_new), h

    xs = tuple(_to_chunks(a, L) for a in (q, k, v, ig, lf))
    (C, n, m), h = lax.scan(chunk, (C0, n0, m0), xs)
    return _from_chunks(h), C, n, m

def _retention(q, k, v, S0):
    L = math.gcd(q.shape[1], CHUNK)
    lg = jnp.log1p(-jnp.exp2(-5.0 - jnp.arange(H_B, dtype=jnp.float32)))
    i = jnp.arange(L, dtype=jnp.float32)
    diff = i[:, None] - i[None, :]
    D = jnp.where(diff >= 0, jnp.exp(jnp.maximum(diff, 0.0) * lg[:, None, None]), 0.0)
    q_dec = jnp.exp((i + 1.0) * lg[:, None])
    k_dec = jnp.exp((L - 1.0 - i) * lg[:, None])
    s_dec = jnp.exp(L * lg)

    def chunk(S, xs):
        qc, kc, vc = xs
        inner = jnp.einsum('bhid,bhjd->bhij', qc, kc) * D
        o = jnp.einsum('bhij,bhje->bhie', inner, vc) + q_dec[..., None] * jnp.einsum('bhid,bhde->bhie', qc, S)
        S = s_dec[:, None, None] * S + jnp.einsum('bhjd,bhje->bhde', kc * k_dec[..., None], vc)
        return S, o

    S, o = lax.scan(chunk, S0, tuple(_to_chunks(a, L) for a in (q, k, v)))
    return _from_chunks(o), S

def _gated_delta(q, k, v, g, beta, S0):
    L = math.gcd(q.shape[1], CHUNK)
    ar = jnp.arange(L)
    strict = ar[:, None] > ar[None, :]
    incl = ar[:, None] >= ar[None, :]
    eye = jnp.eye(L, dtype=jnp.float32)

    def chunk(S, xs):
        qc, kc, vc, gc, bc = xs
        G = jnp.cumsum(gc, axis=-1)
        dec_in = jnp.exp(jnp.where(incl, G[..., :, None] - G[..., None, :], -jnp.inf))
        A = jnp.where(strict, dec_in, 0.0) * bc[..., :, None] * jnp.einsum('bhid,bhjd->bhij', kc, kc)
        gam = jnp.exp(G)
        rhs = jnp.concatenate([(bc * gam)[..., None] * kc, bc[..., None] * vc], axis=-1)
        sol = lax.linalg.triangular_solve(eye + A, rhs, left_side=True, lower=True, unit_diagonal=True)
        W, Ut = sol[..., :HEAD_DIM], sol[..., HEAD_DIM:]
        U = Ut - jnp.einsum('bhid,bhde->bhie', W, S)
        o = gam[..., None] * jnp.einsum('bhid,bhde->bhie', qc, S) + jnp.einsum(
            'bhij,bhje->bhie', jnp.einsum('bhid,bhjd->bhij', qc, kc) * dec_in, U)
        S = jnp.exp(G[..., -1])[..., None, None] * S + jnp.einsum(
            'bhjd,bhje->bhde', kc * jnp.exp(G[..., -1:] - G)[..., None], U)
        return S, o

    S, o = lax.scan(chunk, S0, tuple(_to_chunks(a, L) for a in (q, k, v, g, beta)))
    return _from_chunks(o), S

def _token_mixers(h, pos, st, lp):
    f32 = jnp.float32
    B, T, _ = h.shape
    C0, n0, m0, R0, G0, conv0 = st
    proj = jnp.einsum('btd,de->bte', h, lp['w_in']).astype(f32)
    idx = np.cumsum(IN_SPLITS)[:-1].tolist()
    (qa, ka, va, oa, ia, fa, qb, kb, vb, gb, qc, kc, vc, gcz, ac, bcz) = jnp.split(proj, idx, axis=-1)
    heads = lambda t, H: t.reshape(B, T, H, HEAD_DIM)
    gate_b = lp['mlstm_gate_bias'].astype(f32)

    ig = GATE_SOFTCAP * jnp.tanh((ia + gate_b[:H_A]) / GATE_SOFTCAP)
    lf = jax.nn.log_sigmoid(GATE_SOFTCAP * jnp.tanh((fa + gate_b[H_A:]) / GATE_SOFTCAP))
    ha, C, n, m = _mlstm(heads(qa, H_A), heads(ka, H_A) * HEAD_DIM ** -0.5, heads(va, H_A), ig, lf,
                         C0.astype(f32), n0.astype(f32), m0.astype(f32))
    ya = jax.nn.sigmoid(oa) * _head_norm(ha, lp['norm_mlstm'], False)

    qr = _rotary(heads(qb, H_B), pos)
    kr = _rotary(heads(kb, H_B), pos) * HEAD_DIM ** -0.5
    hb, R = _retention(qr, kr, heads(vb, H_B), R0.astype(f32))
    yb = jax.nn.silu(gb) * _head_norm(hb, lp['norm_ret'], True)

    xc = jnp.concatenate([conv0.astype(f32), jnp.concatenate([qc, kc, vc], axis=-1)], axis=1)
    cw = lp['gdn_conv_w'].astype(f32)
    conv = sum(xc[:, w:w + T] * cw[w] for w in range(CONV_W))
    conv_new = xc[:, xc.shape[1] - (CONV_W - 1):]
    q3, k3, v3 = jnp.split(jax.nn.silu(conv), 3, axis=-1)
    qg = _l2norm(heads(q3, H_C)) * HEAD_DIM ** -0.5
    kg = _l2norm(heads(k3, H_C))
    g = -jnp.exp(lp['gdn_A_log'].astype(f32)) * jax.nn.softplus(ac + lp['gdn_dt_bias'].astype(f32))
    beta = jax.nn.sigmoid(bcz)
    hc, Gs = _gated_delta(qg, kg, heads(v3, H_C), g, beta, G0.astype(f32))
    yc = jax.nn.silu(gcz) * _head_norm(hc, lp['norm_gdn'], False)

    y = jnp.concatenate([ya, yb, yc], axis=-1).astype(h.dtype)
    y = jnp.einsum('bte,ed->btd', y, lp['w_out'])
    return y, (C, n, m, R, Gs, conv_new)

def _layer(x, pos, st, lp):
    h = _rmsnorm(x, lp['norm_mix_pre'])
    y, new_st = _token_mixers(h, pos, st, lp)
    x = x + _rmsnorm(y, lp['norm_mix_post'])
    h = _rmsnorm(x, lp['norm_mlp_pre'])
    u = jnp.square(jax.nn.relu(jnp.einsum('btd,df->btf', h, lp['w_up'])))
    x = x + _rmsnorm(jnp.einsum('btf,fd->btd', u, lp['w_down']), lp['norm_mlp_post'])
    return x, new_st

def setup_inputs(seed: int = 0) -> dict:
    key = jax.random.key(seed)
    ks = jax.random.split(key, 24)
    f32 = jnp.float32
    nrm = lambda k, shape, s: jax.random.normal(k, shape, f32) * s
    gain = lambda k, n: 1.0 + 0.02 * jax.random.normal(k, (DEPTH, n), f32)
    dt = jnp.exp(jax.random.uniform(ks[20], (DEPTH, H_C), f32, math.log(1e-3), math.log(1e-1)))
    gate_bias = jnp.concatenate([
        -1.0 + 0.1 * jax.random.normal(ks[21], (DEPTH, H_A), f32),
        jnp.linspace(3.0, 6.0, H_A, dtype=f32)[None, :] + 0.1 * jax.random.normal(ks[22], (DEPTH, H_A), f32)], axis=-1)
    return {
        'x_prompt': nrm(ks[0], (BATCH, SEQ, D_MODEL), 1.0),
        'x_sample': nrm(ks[1], (DEC_BATCH, DEC_SEQ, D_MODEL), 1.0),
        'state_mlstm_C': nrm(ks[2], (DEPTH, DEC_BATCH, H_A, HEAD_DIM, HEAD_DIM), 0.3),
        'state_mlstm_n': nrm(ks[3], (DEPTH, DEC_BATCH, H_A, HEAD_DIM), 0.3),
        'state_mlstm_m': nrm(ks[4], (DEPTH, DEC_BATCH, H_A), 0.5),
        'state_ret_S': nrm(ks[5], (DEPTH, DEC_BATCH, H_B, HEAD_DIM, HEAD_DIM), 0.5),
        'state_gdn_S': nrm(ks[6], (DEPTH, DEC_BATCH, H_C, HEAD_DIM, HEAD_DIM), 0.1),
        'state_gdn_conv': nrm(ks[7], (DEPTH, DEC_BATCH, CONV_W - 1, 3 * D_C), 1.0),
        'norm_mix_pre': gain(ks[8], D_MODEL),
        'norm_mix_post': gain(ks[9], D_MODEL),
        'norm_mlp_pre': gain(ks[10], D_MODEL),
        'norm_mlp_post': gain(ks[11], D_MODEL),
        'w_in': nrm(ks[12], (DEPTH, D_MODEL, N_IN), D_MODEL ** -0.5),
        'mlstm_gate_bias': gate_bias,
        'gdn_conv_w': nrm(ks[13], (DEPTH, CONV_W, 3 * D_C), CONV_W ** -0.5),
        'gdn_A_log': jnp.log(jax.random.uniform(ks[14], (DEPTH, H_C), f32, 1.0, 16.0)),
        'gdn_dt_bias': dt + jnp.log(-jnp.expm1(-dt)),
        'norm_mlstm': gain(ks[15], D_A),
        'norm_ret': gain(ks[16], D_B),
        'norm_gdn': gain(ks[17], HEAD_DIM),
        'w_out': nrm(ks[18], (DEPTH, D_MIX, D_MODEL), D_MIX ** -0.5),
        'w_up': nrm(ks[19], (DEPTH, D_MODEL, D_FF), D_MODEL ** -0.5),
        'w_down': nrm(ks[23], (DEPTH, D_FF, D_MODEL), D_FF ** -0.5),
    }

def reference(x_prompt, x_sample, state_mlstm_C, state_mlstm_n, state_mlstm_m, state_ret_S, state_gdn_S,
              state_gdn_conv, norm_mix_pre, norm_mix_post, norm_mlp_pre, norm_mlp_post, w_in, mlstm_gate_bias,
              gdn_conv_w, gdn_A_log, gdn_dt_bias, norm_mlstm, norm_ret, norm_gdn, w_out, w_up, w_down):
    f32 = jnp.float32
    bp, tp = x_prompt.shape[:2]
    pos_p = jnp.arange(tp, dtype=jnp.int32)
    pos_s = PAST_LEN + jnp.arange(x_sample.shape[1], dtype=jnp.int32)
    zero_st = (jnp.zeros((bp, H_A, HEAD_DIM, HEAD_DIM), f32), jnp.zeros((bp, H_A, HEAD_DIM), f32),
               jnp.zeros((bp, H_A), f32), jnp.zeros((bp, H_B, HEAD_DIM, HEAD_DIM), f32),
               jnp.zeros((bp, H_C, HEAD_DIM, HEAD_DIM), f32), jnp.zeros((bp, CONV_W - 1, 3 * D_C), f32))
    xp, xs = x_prompt, x_sample
    p_states, s_states = [], []
    for l in range(DEPTH):
        lp = {'norm_mix_pre': norm_mix_pre[l], 'norm_mix_post': norm_mix_post[l],
              'norm_mlp_pre': norm_mlp_pre[l], 'norm_mlp_post': norm_mlp_post[l],
              'w_in': w_in[l], 'mlstm_gate_bias': mlstm_gate_bias[l], 'gdn_conv_w': gdn_conv_w[l],
              'gdn_A_log': gdn_A_log[l], 'gdn_dt_bias': gdn_dt_bias[l], 'norm_mlstm': norm_mlstm[l],
              'norm_ret': norm_ret[l], 'norm_gdn': norm_gdn[l], 'w_out': w_out[l],
              'w_up': w_up[l], 'w_down': w_down[l]}
        xp, st_p = _layer(xp, pos_p, zero_st, lp)
        st_in = (state_mlstm_C[l], state_mlstm_n[l], state_mlstm_m[l], state_ret_S[l], state_gdn_S[l], state_gdn_conv[l])
        xs, st_s = _layer(xs, pos_s, st_in, lp)
        p_states.append(st_p)
        s_states.append(st_s)
    stk = lambda sts, j: jnp.stack([s[j] for s in sts], axis=0)
    return (xp, xs,
            stk(p_states, 0), stk(p_states, 1), stk(p_states, 2), stk(p_states, 3), stk(p_states, 4), stk(p_states, 5),
            stk(s_states, 0), stk(s_states, 1), stk(s_states, 2), stk(s_states, 3), stk(s_states, 4), stk(s_states, 5))


_drawn_inputs = setup_inputs


def setup_inputs(seed=0):
    import zlib

    import numpy as np

    out = dict(_drawn_inputs(seed))
    spreads = {}
    factors = {'norm_mlp_pre': 2.786,
     'norm_mlp_post': 3.193,
     'norm_mlstm': 28.154,
     'norm_ret': 25.849,
     'norm_gdn': 20.699,
     'norm_mix_post': 2.853}
    for name, (base, spread) in spreads.items():
        noise = np.random.default_rng([zlib.crc32(name.encode()), seed]).standard_normal(out[name].shape)
        drawn = base * np.exp(spread * noise) if base else spread * noise
        out[name] = __import__('jax').numpy.asarray(drawn.astype(out[name].dtype))
    for name, factor in factors.items():
        out[name] = (out[name] * factor).astype(out[name].dtype)
    return out
```

```python
from contextlib import ExitStack

import numpy as np

import concourse.bass as bass
from concourse import mybir

F32 = mybir.dt.float32
F32R = mybir.dt.float32r
ACT = mybir.ActivationFunctionType
ALU = mybir.AluOpType

DEPTH = 2
D_MODEL = 2048
D_FF = 4 * D_MODEL
HD = 128
SEQ = 256
NB = 8
DS = 4
NS = NB * DS
T = SEQ + NS
TILES = ((0, 128, 128), (128, 256, 128), (256, 288, 32))
NC_ = D_MODEL // HD
H_C, H_B, H_A = 8, 4, 4
HEADS = H_C + H_B + H_A
SCALE = HD ** -0.5
EPS = 1e-6
SOFTCAP = 15.0
PAST_LEN = 2048
CONVW = 4
QUADS = HEADS + NC_ // 4 + 2 * D_FF // HD // 4
MLP_Q = D_FF // D_MODEL
SLOTS = 32
LEVELS = 7
BIG = -1e30
CAP = 2.0 ** 62
CB_P = SEQ + CONVW - 1
CB_N = CB_P + NB * (DS + CONVW - 1)
CO = CB_N - (CONVW - 1)
EXT_P = SEQ + 1
EXT = EXT_P + NB * (DS + 1)
AUX_GAIN, AUX_TAP, AUX_STATE = 0, 1, 16
AUXW = AUX_STATE + T
CONVS = 3 * NB * (CONVW - 1)
BCW = 2 * T + NS


def shape_constants():
    f = np.float32
    half = HD // 2
    inv = np.power(f(10000.0), -np.arange(half, dtype=f) / f(half)).astype(f)
    pos = np.concatenate([np.arange(SEQ), np.tile(PAST_LEN + np.arange(DS), NB)]).astype(f)
    ang = (pos[None, :] * inv[:, None]).astype(f)
    cos, sin = np.cos(ang).astype(f), np.sin(ang).astype(f)
    ident = np.eye(HD, dtype=f)
    rot = np.zeros((HD, HD), f)
    rot[np.arange(half) + half, np.arange(half)] = -1.0
    rot[np.arange(half), np.arange(half) + half] = 1.0
    i = np.arange(HD)
    seq = np.arange(NS) // DS
    causal = (i[None, :] >= i[:, None]).astype(f)
    causal_s = np.zeros((HD, NS), f)
    causal_s[:NS] = (seq[None, :] == seq[:, None]) * (np.arange(NS)[None, :] >= np.arange(NS)[:, None])
    own = np.zeros((HD, NB), f)
    own[np.arange(NS), seq] = 1.0
    levels = np.stack([((i[:, None] // (2 * b) == i[None, :] // (2 * b)) & (i[:, None] % (2 * b) < b)
                        & (i[None, :] % (2 * b) >= b)).astype(f) for b in (2 ** n for n in range(LEVELS))], 1)
    lg = np.log1p(-np.exp2(-5.0 - np.arange(H_B, dtype=np.float64)))
    t = np.arange(SEQ)
    dmat = np.zeros((HD, H_B, T), f)
    kdec = np.zeros((HD, H_B, 3), f)
    rdec = np.zeros((HD, H_B, NS), f)
    for h in range(H_B):
        dist = t[None, :] - i[:, None]
        dmat[:, h, :SEQ] = np.where(dist >= 0, np.exp(np.maximum(dist, 0) * lg[h]), 0.0)
        ds = np.arange(NS)[None, :] - np.arange(NS)[:, None]
        dmat[:NS, h, SEQ:] = causal_s[:NS] * np.exp(np.maximum(ds, 0) * lg[h])
        kdec[:, h, 0] = np.exp((SEQ - 1 - i) * lg[h]) * SCALE
        kdec[:, h, 1] = np.exp((HD - 1 - i) * lg[h]) * SCALE
        kdec[:NS, h, 2] = np.exp((DS - 1 - np.arange(NS) % DS) * lg[h]) * SCALE
        rdec[:, h] = np.exp((np.arange(NS) % DS + 1) * lg[h])
    resets = np.ones((HD, T), f)
    resets[:, 0] = 0.0
    resets[:, SEQ::DS] = 0.0
    resets[64:, HD] = 0.0
    rows = np.zeros((H_B, BCW), f)
    rows[:, 2 * T:] = rdec[0]
    return {
        "k_rows": rows, "k_kdec": kdec,
        "c_ident": ident, "c_rot": rot, "c_center": ident - f(1.0 / HD), "c_causal": causal,
        "c_never": (1.0 - causal) * f(BIG), "c_causal_s": causal_s, "c_never_s": (1.0 - causal_s) * f(BIG),
        "c_own": own, "c_levels": levels, "c_cos": np.concatenate([cos, cos]), "c_sin": np.concatenate([sin, sin]),
        "k_dmat": dmat, "k_resets": resets,
    }


def build(nc, d):
    with ExitStack() as ctx:
        def sb(name, shape, dt=F32):
            return ctx.enter_context(nc.sbuf_tensor(name, shape, dt))

        sems = {}

        def sem(name):
            if name not in sems:
                sems[name] = ctx.enter_context(nc.semaphore(name))
            return sems[name]

        X = sb("X", [128, NC_, T])
        Y = sb("Y", [128, NC_, T])
        HH, HL = sb("HH", [128, NC_, T], F32R), sb("HL", [128, NC_, T], F32R)
        UH, UL = sb("UH", [128, NC_, T], F32R), sb("UL", [128, NC_, T], F32R)
        RAW = [sb(f"RAW{i}", [128, NC_ // 4, HD]) for i in range(4)]
        WH = [sb(f"WH{i}", [128, NC_, HD], F32R) for i in range(2)]
        WL = [sb(f"WL{i}", [128, NC_, HD], F32R) for i in range(2)]
        con = {n: sb(n, list(d[n].shape)) for n in d if n.startswith("c_")}
        IDENT, OWN = con["c_ident"], con["c_own"]
        ONES = sb("ONES", [128, HD])
        S, RS = sb("S", [128, T]), sb("RS", [128, T])
        EPSC = sb("EPSC", [128, 1])
        ONEC = sb("ONEC", [128, 1])
        NG = sb("NG", [128, 4, NC_])
        GP = sb("GP", [128, 2])
        MI = sb("MI", [H_A, NB])
        Z = [sb(f"Z{i}", [128, 4, T]) for i in range(2)]
        AUX = [sb(f"AUX{i}", [128, AUXW]) for i in range(2)]
        BC = [sb(f"BC{i}", [128, BCW]) for i in range(2)]
        SIN = sb("SIN", [128, NB, HD])
        SOUT = sb("SOUT", [128, HD])
        NOUT = sb("NOUT", [128, 1 + NB])
        CNEW = sb("CNEW", [128, 3, (1 + NB) * (CONVW - 1)])
        MOUT = sb("MOUT", [H_A, 1 + NB])
        COLA, COLB = sb("COLA", [128, 3, 128]), sb("COLB", [128, 3, 128])
        CUR = sb("CUR", [128, 3, 3])
        ybase = [0]

        def scratch(shape):
            n = int(np.prod(shape[1:]))
            a = Y[0:shape[0]].rearrange("p c t -> p (c t)")[:, ybase[0]:ybase[0] + n]
            ybase[0] += n
            if len(shape) == 3:
                a = a.rearrange("p (a b) -> p a b", b=shape[2])
            return a

        CDEC = scratch([128, NB, HD])
        VEXP = scratch([128, NB, HD])
        TR = scratch([128, 4, HD])
        V_ = scratch([128, 3, HD])
        KW = scratch([128, 3, HD])
        U_ = scratch([128, 3, HD])
        QK2 = scratch([128, 2, T])
        DX = scratch([128, T])
        assert ybase[0] <= NC_ * T
        CB = sb("CB", [128, 3, CB_N])
        AE = sb("AE", [128, 6, CO])
        ACC, EE = AE[:, 0:3], AE[:, 3:6]
        QKG = sb("QKG", [128, 2, T])
        AM = sb("AM", [128, T])
        SC = sb("SC", [128, 416])
        PM = sb("PM", [128, T])
        S1 = sb("S1", [128, HD])
        RHS = sb("RHS", [128, 2, HD])
        TS = sb("TS", [NS, 2, NS])
        SMALL = sb("SMALL", [128, 2, NS])
        SQH, LG, GATE = [sb(n, [128, T]) for n in ("SQH", "LG", "GATE")]
        HHD, YY = AM, PM
        LW = EE.rearrange("p a b -> p (a b)")[:, 0:416]
        SQ = AE[:].rearrange("p a b -> p (a b)")[:, 0:4 * T].rearrange("p (a b) -> p a b", b=T)
        GWf = Y[:].rearrange("p c t -> p (c t)")[:, 0:NC_ * HD].rearrange("p (c m) -> p c m", m=HD)
        RESETS = Y[:].rearrange("p c t -> p (c t)")[:, 2560:2560 + T]
        ZG, GE, GT, GU = ACC[:, 0, 0:T], ACC[:, 1, 0:T], EE[:, 0, 0:T], QKG[:, 0]
        ROWA, ROWB = Z[1][:, 3], QK2[:, 0]
        AR, EM, IR = [Z[1][0:H_A, j] for j in range(3)]
        EXTF, EXTI, EXTM = [CB[0:H_A, j, 0:EXT] for j in range(3)]
        F0, MC = QKG[0:H_A, 1], AM[0:H_A, :]
        UPE = [ACC[:, 0, 0:T], ACC[:, 1, 0:T]]
        UPT = [EE[:, 0, 0:T], EE[:, 1, 0:T]]

        PU = [ctx.enter_context(nc.psum_tensor(f"PU{i}", [128, 512], F32)) for i in range(2)]
        PAB = ctx.enter_context(nc.psum_tensor("PAB", [128, 2, 512], F32))
        PCD = ctx.enter_context(nc.psum_tensor("PCD", [128, 2, 512], F32))
        PE_ = ctx.enter_context(nc.psum_tensor("PE_", [128, 512], F32))
        PF = ctx.enter_context(nc.psum_tensor("PF", [128, 512], F32))
        PA, PB, PC, PD = PAB[:, 0], PAB[:, 1], PCD[:, 0], PCD[:, 1]
        print("sbuf left", nc.sbuf_bytes_remaining() if callable(nc.sbuf_bytes_remaining) else nc.sbuf_bytes_remaining)

        def sview(a):
            return a[:, SEQ:T].rearrange("p (b t) -> p b t", t=DS)

        def walk(eng, start, quad, mix_alone, after_out, after_mlp):
            with eng.Fori(0, DEPTH) as l:
                q0, n0, p0 = l * QUADS, l * HEADS, l * (HEADS // 2)
                start(l)
                quad(q0, "first", l, None)
                with eng.Fori(0, H_C // 2) as i:
                    for par in range(2):
                        h = 2 * i + par
                        quad(q0 + 1 + h, "gdn", l, (n0 + h, l * H_C + h, h, par, p0 + i))
                with eng.Fori(0, H_B // 2) as i:
                    for par in range(2):
                        h = 2 * i + par
                        quad(q0 + 1 + H_C + h, "ret", l, (n0 + H_C + h, l * H_B + h, h, par, p0 + H_C // 2 + i))
                for h in range(H_A - 1):
                    quad(q0 + 1 + H_C + H_B + h, "mls", l, (n0 + H_C + H_B + h, l * H_A + h, h, h % 2, p0 + (H_C + H_B + h) // 2))
                h = H_A - 1
                mix_alone("mls", l, (n0 + H_C + H_B + h, l * H_A + h, h, h % 2, p0 + (H_C + H_B + h) // 2))
                with eng.Fori(0, NC_ // 4) as j:
                    quad(q0 + HEADS + j, "out", l, (0, j))
                after_out(l)
                base = q0 + HEADS + NC_ // 4
                with eng.Fori(0, NC_ // 4) as j:
                    quad(base + j, "up", l, (0, j))
                with eng.Fori(0, NC_ // 4) as j:
                    quad(base + 4 + j, "down0", l, (0, j))
                with eng.Fori(0, MLP_Q - 1) as q:
                    with eng.Fori(0, NC_ // 4) as j:
                        quad(base + 8 + 8 * q + j, "up", l, (q + 1, j))
                    with eng.Fori(0, NC_ // 4) as j:
                        quad(base + 12 + 8 * q + j, "down", l, (q + 1, j))
                after_mlp(l)

        def ul_before(l, kind, q):
            return l * (NC_ * (1 + MLP_Q)) + (0 if kind == "out" else NC_ * (q + 1))

        gate_steps = {
            "pe": ["proj", "turned"],
            "act": ["rate", "tanh_exp", "beta_exp", "sp_exp", "log", "gamma", "kd_exp", "em", "wl_exp", "inter"],
            "dve": ["weights", "z", "biased", "tanh_sum", "tanh_rec", "capped", "beta_sum", "beta", "y", "abs", "u", "rest",
                    "log1p", "softplus", "decay", *["ext"] * 4, "ext_f", *["ext"] * 2, *["scan"] * 2, "i", "f", *["m"] * 2,
                    "sums", *["mout"] * 2, "rows", *["kd_log"] * 3, "a", "b", *["wl_log"] * 2, "inter_log", "wl",
                    *["cols"] * 4],
        }

        def gate(name, l):
            engine = next(e for e, steps in gate_steps.items() if name in steps)
            steps = gate_steps[engine]
            return sem(f"gate_steps_{engine}"), l * len(steps) + len(steps) - steps[::-1].index(name)

        def aux_count(kind, x):
            n, nk, hk, par, pair = x
            return 16 * (pair + 1)

        def up_units(l, x, s):
            q, j = x
            return (l * MLP_Q + q) * NC_ + 4 * j + s

        block = ctx.enter_context(nc.Block())

        @block.sync
        def _(sp):
            sp.dma_start(X[:], d["x"]).then_inc(sem("x_in"), 16)
            for n in con:
                sp.dma_start(con[n][:], d[n]).then_inc(sem("constants_in"), 16)

            def load(c, unit):
                k = slice(4 * c, 4 * c + 4)
                src = d["w"][unit, :, k] if isinstance(unit, int) else d["w"][bass.ds(unit, 1), :, k].rearrange("a p k m -> p (a k) m")
                sp.dma_start(RAW[c][:], src).then_inc(sem(f"raw_in{c}"), 16)

            for c in range(4):
                load(c, 0)
            with sp.Fori(0, DEPTH * QUADS) as Q:
                for s in range(4):
                    for c in range(4):
                        sp.wait_ge(sem("lo_ready"), 16 * Q + 4 * s + c + 1)
                        load(c, 4 * Q + s + 1)
            sp.wait_ge(sem("lo_ready"), 16 * DEPTH * QUADS + 1)
            load(0, 4 * DEPTH * QUADS + 1)
            sp.wait_ge(sem("x_final"), DEPTH)
            sp.dma_start(d["y"], X[:]).then_inc(sem("y_stored"), 16)
            sp.wait_ge(sem("y_stored"), 16)

        @block.gpsimd
        def _(pool):
            def held(name, value):
                pool.wait_ge(sem(name) if isinstance(name, str) else name, value)
                pool.sem_inc(sem("pool_passes"), 1)

            def one(name, n):
                a = d[name][bass.ds(n, 1)]
                return a.rearrange("a p w -> p (a w)")

            def load_head(n, par, pairs):
                pool.dma_start(AUX[par][:], one("aux", n)).then_inc(sem(f"aux_in{par}"), 16)
                pool.dma_start(BC[par][:], d["bc"][bass.ds(n, 1)].rearrange("a t -> (a t)")
                               .partition_broadcast(128)).then_inc(sem(f"bc_in{par}"), 16)

            def load_state(n):
                pool.dma_start(SIN[:].rearrange("p b e -> p (b e)"), one("sin", n)).then_inc(sem("state_in"), 16)

            def head(l, n, pair, par, next_head):
                if next_head:
                    held("head_done", n + 1)
                    load_head(n + 1, 1 - par, pair)
                pool.wait_ge(sem(f"bc_in{par}"), 16 * (pair + 1))
                pool.wait_ge(sem("state_in"), 16 * (n + 1))
                pool.wait_ge(sem("state_ready"), n + 1)
                dec = BC[par][:, 2 * T + DS - 1:BCW:DS].unsqueeze(2).to_broadcast([128, NB, HD])
                pool.tensor_tensor(CDEC, SIN[:], dec, ALU.mult).then_inc(sem("state_decayed"), 1)
                pool.wait_ge(sem("sample_values"), n + 1)
                pool.tensor_tensor(VEXP[0:NS], U_[0:NS, 2].unsqueeze(1).to_broadcast([NS, NB, HD]),
                                   OWN[0:NS].unsqueeze(2).to_broadcast([NS, NB, HD]), ALU.mult).then_inc(sem("values_spread"), 1)
                if next_head:
                    held("state_decayed", n + 1)
                    held("state_read", n + 1)
                    load_state(n + 1)
                held("state_ready", n + 2)
                pool.dma_start(one("sout", n)[:, HD:], CDEC.rearrange("p b e -> p (b e)")).then_inc(sem("state_out"), 16)
                held("state_out", 16 * (n + 1))

            held("constants_in", 16 * len(con))
            for name in ("prompt_out", "norm_out", "cnew_out"):
                pool.sem_inc(sem(name), 16)
            for l in range(DEPTH):
                pool.dma_start(d["bc"][l * HEADS + H_C:l * HEADS + H_C + H_B], d["k_rows"]).then_inc(sem("ret_rows_out"), 16)
            held("ret_rows_out", 16 * DEPTH)
            with pool.Fori(0, DEPTH) as l:
                n0, p0 = l * HEADS, l * (HEADS // 2)
                held("layer_free", l + 1)
                pool.dma_start(NG[:].rearrange("p k c -> p (k c)"), one("ng", l)).then_inc(sem("gains_in"), 16)
                pool.dma_start(GP[:], one("gp", l)).then_inc(sem("gate_in"), 16)
                pool.dma_start(MI[:], one("mi", l)).then_inc(sem("gate_in"), 16)
                pool.dma_start(RESETS, d["k_resets"]).then_inc(sem("gate_in"), 16)
                pool.dma_start(GWf, d["gw"][bass.ds(l, 1)].rearrange("a p c m -> p (a c) m")).then_inc(sem("gate_in"), 16)
                held(*gate("em", l))
                held(*gate("inter", l))
                held(*gate("a", l))
                held(*gate("rows", l))
                held(*gate("gamma", l))
                held(*gate("mout", l))
                a0 = n0 + H_C + H_B
                rows_a, rows_c = d["bc"][bass.ds(a0, H_A)], d["bc"][bass.ds(n0, H_C)]
                pool.dma_start(rows_a[:, 0:T], AR[:]).then_inc(sem("rows_out"), 16)
                pool.dma_start(rows_a[:, T:2 * T], EM[:]).then_inc(sem("rows_out"), 16)
                pool.dma_start(rows_a[:, 2 * T:], IR[:, SEQ:T]).then_inc(sem("rows_out"), 16)
                pool.dma_start(rows_c[:, 0:T], ROWA[64:64 + H_C]).then_inc(sem("rows_out"), 16)
                pool.dma_start(rows_c[:, T:2 * T], GT[64:64 + H_C]).then_inc(sem("rows_out"), 16)
                pool.dma_start(rows_c[:, 2 * T:], GT[64:64 + H_C, SEQ:T]).then_inc(sem("rows_out"), 16)
                pool.dma_start(one("mo", l), MOUT[:]).then_inc(sem("rows_out"), 16)
                held("rows_out", 16 * 7 * (l + 1))
                load_head(n0, 0, p0)
                load_state(n0)
                with pool.Fori(0, (H_C + H_B) // 2) as i:
                    for par in range(2):
                        head(l, n0 + 2 * i + par, p0 + i, par, True)
                for h in range(H_A):
                    head(l, a0 + h, p0 + (H_C + H_B) // 2 + h // 2, h % 2, h < H_A - 1)
            pool.wait_ge(sem("state_out"), 16 * DEPTH * HEADS)
            pool.wait_ge(sem("rows_out"), 16 * 7 * DEPTH)

        @block.tensor
        def _(pe):
            pe.wait_ge(sem("constants_in"), 16 * len(con))

            def mm(out, lhsT, rhs, start=True, stop=True):
                return nc.tensor.matmul(out, lhsT, rhs, start=start, stop=stop, skip_group_check=True)

            def transpose(out, in_):
                return nc.tensor.matmul(out, in_, IDENT[:], is_transpose=True, start=True, stop=True, skip_group_check=True)

            def unit_part(Q, t, kind, l, x):
                s, kk = divmod(t, 8)
                hi, lo = (UH, UL) if kind in ("out", "down", "down0") else (HH, HL)
                if kk == 0:
                    pe.wait_ge(sem("psum_read"), 4 * Q + s + 1)
                if kk % 2 == 0:
                    pe.wait_ge(sem("lo_ready"), 16 * Q + 4 * s + kk // 2 + 1)
                for k in (2 * kk, 2 * kk + 1):
                    if s == 0:
                        if kind == "first":
                            pe.wait_ge(sem("hl_ready"), 2 * l * NC_ + k + 1)
                        elif kind in ("out", "down", "down0"):
                            pe.wait_ge(sem("ul_ready"), ul_before(l, kind, x[0]) + k + 1)
                        elif kind == "up":
                            pe.wait_ge(sem("hl_ready"), (2 * l + 1) * NC_ + k + 1)
                    mm(PU[s % 2][:, 0:T], WH[s % 2][:, k], hi[:, k], k == 0, False)
                    mm(PU[s % 2][:, 0:T], WH[s % 2][:, k], lo[:, k], False, False)
                    last = mm(PU[s % 2][:, 0:T], WL[s % 2][:, k], hi[:, k], False, k == NC_ - 1)
                if kk == 7:
                    last.then_inc(sem("unit_done"), 1)

            def norm_sums(e):
                for c in range(NC_):
                    pe.wait_ge(sem("squares"), NC_ * e + c + 1)
                    mm(PC[:, 0:T], ONES[:], SQ[:, c % 4], c == 0, c == NC_ - 1).then_inc(sem("squares_summed"), 1)

            def gates(t, l):
                if 8 <= t < 24:
                    k = t - 8
                    if k == 0:
                        pe.wait_ge(*gate("weights", l))
                    i = mm(PD[:, 0:T], GWf[:, k], X[:, k], k == 0, k == NC_ - 1)
                    if k == NC_ - 1:
                        i.then_inc(gate("proj", 0)[0], 1)
                if t == 31:
                    pe.wait_ge(*gate("wl", l))
                    pe.wait_ge(*gate("beta", l))
                    pe.wait_ge(*gate("kd_exp", l))
                    pe.wait_ge(*gate("rows", l))
                    pe.wait_ge(*gate("b", l))
                    for dst, src in ((PE_, ROWA), (PF, ROWB)):
                        for j, (a, b, m) in enumerate(TILES):
                            i = mm(dst[0:m, j * HD:(j + 1) * HD], src[:, a:b], IDENT[:])
                    i.then_inc(gate("turned", 0)[0], 1)

            def linear_head(t, kind, x):
                n, nk, hk, par, pair = x
                mls = kind == "mls"
                z = Z[par]
                q, k = (z[:, 0], z[:, 1]) if mls else (QK2[:, 0], QK2[:, 1])
                v = z[:, 2]
                if t == 0:
                    pe.wait_ge(sem("head_done"), n + 1)
                if t == 0 and not mls:
                    pe.wait_ge(sem("z_ready"), 4 * n + 4)
                    mm(PC[:, 0:T], con["c_rot"][:], z[:, 0])
                    mm(PD[:, 0:T], con["c_rot"][:], z[:, 1]).then_inc(sem("ret_rotated"), 1)
                if t == 2:
                    if mls:
                        pe.wait_ge(sem("z_ready"), 4 * n + 4)
                    else:
                        pe.wait_ge(sem("ret_qk"), 3 * (nk + 1))
                    pe.wait_ge(sem("state_ready"), n + 1)
                    for dst, src in ((PA, k), (PB, v)):
                        for j, (a, b, m) in enumerate(TILES):
                            last = mm(dst[0:m, j * HD:(j + 1) * HD], src[:, a:b], IDENT[:])
                    last.then_inc(sem("kv_turned"), 1)
                    mm(PE_[:, 0:SEQ], k[:, 0:HD], q[:, 0:SEQ])
                    mm(PE_[:, SEQ:SEQ + HD], k[:, HD:SEQ], q[:, HD:SEQ])
                    mm(PE_[0:NS, 384:416], k[:, SEQ:T], q[:, SEQ:T]).then_inc(sem("scores"), 1)
                if t == 3:
                    pe.wait_ge(sem(f"{kind}_probs"), (2 if mls else 3) * (nk + 1))
                    pe.wait_ge(sem(f"{kind}_kept"), 5 * (nk + 1))
                    pe.wait_ge(sem(f"{kind}_qs"), nk + 1)
                    pe.wait_ge(sem("state_in"), 16 * (n + 1))
                    mm(PF[:, 0:SEQ], U_[:, 0], SC[:, 0:SEQ], True, False)
                    mm(PF[:, HD:SEQ], U_[:, 1], SC[:, SEQ:SEQ + HD], False, False)
                    for b in range(NB):
                        c = slice(SEQ + DS * b, SEQ + DS * b + DS)
                        i = mm(PF[:, c], SIN[:, b], SMALL[:, 0, DS * b:DS * b + DS], False, False)
                    i.then_inc(sem("state_read"), 1)
                    i = mm(PF[:, SEQ:T], U_[0:NS, 2], SC[0:NS, 384:416], False, True)
                    if mls:
                        pe.wait_ge(sem("mls_qn"), nk + 1)
                        mm(PC[:, 0:SEQ], ONES[:], SC[:, 0:SEQ], True, False)
                        mm(PC[:, HD:SEQ], ONES[:], SC[:, SEQ:SEQ + HD], False, False)
                        mm(PC[:, SEQ:T], ONES[:], SMALL[:, 1], False, False)
                        i = mm(PC[:, SEQ:T], ONES[0:NS], SC[0:NS, 384:416], False, True)
                    i.then_inc(sem(f"{kind}_out"), 1)
                    mm(PD[:, 0:HD], KW[:, 0], U_[:, 0], True, False)
                    i = mm(PD[:, 0:HD], KW[:, 1], U_[:, 1], False, True)
                    if mls:
                        mm(PD[:, HD:HD + 1], KW[:, 0], ONES[:, 0:1], False, False)
                        mm(PD[:, HD:HD + 1], KW[:, 1], ONES[:, 0:1], False, True)
                        i = mm(PD[:, HD + 1:HD + 1 + NB], KW[0:NS, 2], OWN[0:NS], False, True)
                    i.then_inc(sem("prompt_state"), 1)
                if t == 4 and not mls:
                    pe.wait_ge(sem("ret_kept_out"), nk + 1)
                    mm(PC[:, 0:T], con["c_center"][:], YY[:]).then_inc(sem("ret_centered"), 1)
                if t == 8:
                    if mls:
                        pe.wait_ge(sem("mls_nout"), 3 * (nk + 1))
                    head_sums(n)
                if t == 10:
                    sample_state(n)

            def head_sums(n):
                pe.wait_ge(sem("head_squares"), n + 1)
                pe.wait_ge(sem("state_kept"), n + 1)
                mm(PD[:, 0:T], ONES[:], SQH[:]).then_inc(sem("head_sums"), 1)

            def sample_state(n):
                pe.wait_ge(sem("values_spread"), n + 1)
                mm(PA, KW[0:NS, 2], VEXP[0:NS, 0:4].rearrange("p b e -> p (b e)"))
                mm(PB, KW[0:NS, 2], VEXP[0:NS, 4:8].rearrange("p b e -> p (b e)")).then_inc(sem("sample_state"), 1)

            def gdn_head(t, x):
                n, nk, hk, par, pair = x
                v = Z[par][:, 2]
                if t == 6:
                    pe.wait_ge(sem("gdn_squares"), nk + 1)
                    pe.wait_ge(sem("head_done"), n + 1)
                    mm(PC[:, 0:T], ONES[:], EE[:, 0, 0:T])
                    mm(PD[:, 0:T], ONES[:], EE[:, 1, 0:T]).then_inc(sem("gdn_sums"), 1)
                if t == 8:
                    pe.wait_ge(sem("gdn_qk"), nk + 1)
                    pe.wait_ge(sem("state_ready"), n + 1)
                    q, k = QK2[:, 0], QK2[:, 1]
                    for dst, src in ((PA, k), (PB, v)):
                        for j, (a, b, m) in enumerate(TILES):
                            last = mm(dst[0:m, j * HD:(j + 1) * HD], src[:, a:b], IDENT[:])
                    last.then_inc(sem("kv_turned"), 1)
                    for a, b, m in TILES:
                        i = mm(PC[0:m, a:b], k[:, a:b], k[:, a:b])
                    i.then_inc(sem("gdn_kk"), 1)
                    for a, b, m in TILES:
                        i = mm(PF[0:m, a:b], k[:, a:b], q[:, a:b])
                    i.then_inc(sem("scores"), 1)
                if 9 <= t < 9 + 2 * LEVELS:
                    lev, second = divmod(t - 9, 2)
                    R = [IDENT[:], IDENT[:]] if lev == 0 else [TR[:, 1], TR[:, 3]]
                    TT = [IDENT[:], IDENT[:]] if lev == 0 else [TR[:, 0], TR[:, 2]]
                    Rs = IDENT[0:NS, 0:NS] if lev == 0 else TS[:, 1]
                    Ts = IDENT[0:NS, 0:NS] if lev == 0 else TS[:, 0]
                    if not second:
                        if lev == 0:
                            pe.wait_ge(sem("gdn_A"), 3 * (nk + 1))
                        else:
                            pe.wait_ge(sem("gdn_inverse"), LEVELS * nk + lev)
                        for j in range(2):
                            i = mm(PD[:, j * HD:(j + 1) * HD], AM[:, j * HD:(j + 1) * HD], R[j])
                        if lev < 2:
                            i = mm(PD[0:NS, SEQ:T], AM[0:NS, SEQ:T], Rs)
                        i.then_inc(sem("gdn_P"), 1)
                    else:
                        pe.wait_ge(sem("gdn_Pm"), LEVELS * nk + lev + 1)
                        for j in range(2):
                            p = PM[:, j * HD:(j + 1) * HD]
                            mm(PE_[:, 2 * j * HD:(2 * j + 1) * HD], p, TT[j])
                            i = mm(PE_[:, (2 * j + 1) * HD:(2 * j + 2) * HD], TT[j], p)
                        if lev < 2:
                            mm(PC[0:NS, 0:NS], PM[0:NS, SEQ:T], Ts)
                            i = mm(PC[0:NS, NS:2 * NS], Ts, PM[0:NS, SEQ:T])
                        i.then_inc(sem("gdn_TR"), 1)
                if t == 23:
                    pe.wait_ge(sem("gdn_inverse"), LEVELS * (nk + 1))
                    pe.wait_ge(sem("gdn_kept"), 6 * (nk + 1))
                    mm(PA[:, 0:HD], TR[:, 1], V_[:, 0]).then_inc(sem("gdn_u0"), 1)
                    pe.wait_ge(sem("state_in"), 16 * (n + 1))
                    for b in range(NB):
                        out = PF[:, SEQ + DS * b:SEQ + DS * b + 2 * NS].rearrange("p (a c) -> p a c", c=NS)[:, :, 0:DS]
                        i = mm(out, SIN[:, b], QKG[:, :, SEQ + DS * b:SEQ + DS * b + DS], b == 0, False)
                    i.then_inc(sem("state_read"), 1)
                if t == 24:
                    pe.wait_ge(sem("gdn_u0_kept"), nk + 1)
                    mm(PB[:, 0:HD], KW[:, 0], U_[:, 0]).then_inc(sem("gdn_s1"), 1)
                    pe.wait_ge(sem("gdn_ks_kept"), nk + 1)
                    mm(PC[0:NS, 0:HD], SMALL[:, 0], IDENT[:]).then_inc(sem("gdn_ks_turned"), 1)
                if t == 25:
                    pe.wait_ge(sem("gdn_s1_kept"), nk + 1)
                    pe.wait_ge(sem("gdn_rhs_s"), nk + 1)
                    mm(PB[:, HD:2 * HD], QKG[:, 1, HD:SEQ], S1[:]).then_inc(sem("gdn_ks"), 1)
                    mm(PC[0:NS, HD:2 * HD], TS[:, 1], RHS[0:NS, 1]).then_inc(sem("gdn_us"), 1)
                if t == 26:
                    pe.wait_ge(sem("gdn_rhs"), nk + 1)
                    mm(PA[:, HD:2 * HD], TR[:, 3], RHS[:, 0]).then_inc(sem("gdn_u1"), 1)
                if t == 27:
                    pe.wait_ge(sem("gdn_u1_kept"), nk + 1)
                    mm(PB[:, 2 * HD:3 * HD], KW[:, 1], U_[:, 1]).then_inc(sem("prompt_state"), 1)
                    mm(PF[:, 0:HD], U_[:, 0], SC[:, 0:HD], False, False)
                    mm(PF[:, HD:SEQ], S1[:], QKG[:, 0, HD:SEQ], False, False)
                    mm(PF[:, HD:SEQ], U_[:, 1], SC[:, HD:SEQ], False, False)
                    pe.wait_ge(sem("sample_values"), n + 1)
                    mm(PF[:, SEQ:T], U_[0:NS, 2], SC[0:NS, SEQ:T], False, True).then_inc(sem("gdn_out"), 1)
                if t == 29:
                    head_sums(n)
                if t == 30:
                    pe.wait_ge(sem("state_kept"), n + 1)
                    sample_state(n)

            def mixer(t, kind, l, x):
                if kind == "gdn":
                    gdn_head(t, x)
                elif kind in ("ret", "mls"):
                    linear_head(t, kind, x)
                elif kind == "first":
                    gates(t, l)

            def quad(Q, kind, l, x):
                for t in range(SLOTS):
                    unit_part(Q, t, kind, l, x)
                    mixer(t, kind, l, x)

            def mix_alone(kind, l, x):
                for t in range(SLOTS):
                    mixer(t, kind, l, x)

            pe.sem_inc(sem("unit_done"), 2)
            pe.sem_inc(sem("psum_read"), 2)
            pe.wait_ge(sem("x_in"), 16)
            pe.wait_ge(sem("ones_set"), 1)

            def after_out(l):
                norm_sums(4 * l + 1)
                norm_sums(4 * l + 2)

            walk(pe, lambda l: norm_sums(4 * l), quad, mix_alone, after_out, lambda l: norm_sums(4 * l + 3))

        @block.scalar
        def _(act):
            act.preload_act_table_set("natural_log_exp_and_others")

            def fn(out, in_, f=ACT.Copy, **kw):
                return nc.scalar.activation(out, in_, f, **kw)

            def hi_part(Q, p):
                s, c = divmod(p, 4)
                act.wait_ge(sem(f"raw_in{c}"), 16 * (4 * Q + s + 1))
                if c == 0:
                    act.wait_ge(sem("unit_done"), 4 * Q + s + 1)
                k = slice(4 * c, 4 * c + 4)
                fn(WH[s % 2][:, k], RAW[c][:]).then_inc(sem("hi_ready"), 1)

            def prenorm(l, e, gain):
                act.wait_ge(sem("gains_in"), 16 * (l + 1))
                for c in range(NC_):
                    if e == 0:
                        act.wait_ge(sem("x_in"), 16)
                        if c == 0:
                            act.wait_ge(sem("layer_free"), l + 1)
                    else:
                        act.wait_ge(sem("x_updated"), 8 * l + c // 4 + 1)
                    fn(HH[:, c], X[:, c], scale=NG[:, gain, c:c + 1]).then_inc(sem("hh_ready"), 1)
                squares(4 * l + e, X)
                norm_scale(4 * l + e, S, "s_ready")

            def squares(e, src):
                for c in range(NC_):
                    if c >= 4:
                        act.wait_ge(sem("squares_summed"), NC_ * e + c - 3)
                    fn(SQ[:, c % 4], src[:, c], ACT.Square).then_inc(sem("squares"), 1)

            def norm_scale(e, dst, name):
                act.wait_ge(sem("squares_summed"), NC_ * (e + 1))
                fn(dst[:], PC[:, 0:T], ACT.Ln, scale=1.0 / D_MODEL, bias=EPSC[:, 0:1]).then_inc(sem("norm_log"), 1)
                act.wait_ge(sem("norm_log"), e + 1)
                fn(dst[:], dst[:], ACT.Exp, scale=-0.5).then_inc(sem(name), 1)

            def gates(t, l):
                if t == 22:
                    act.wait_ge(sem("gate_in"), 16 * 4 * (l + 1))
                    fn(GP[:, 1:2], GP[:, 1:2], ACT.Exp).then_inc(gate("rate", 0)[0], 1)
                if t == 24:
                    act.wait_ge(*gate("biased", l))
                    fn(GE[0:64], ZG[0:64], ACT.Exp, scale=2.0 / SOFTCAP).then_inc(gate("tanh_exp", 0)[0], 1)
                    fn(ROWA[96:128], ZG[96:128], ACT.Exp, scale=-1.0).then_inc(gate("beta_exp", 0)[0], 1)
                if t == 25:
                    act.wait_ge(*gate("abs", l))
                    fn(GE[:], GE[:], ACT.Exp, scale=-1.0).then_inc(gate("sp_exp", 0)[0], 1)
                    act.wait_ge(*gate("rest", l))
                    fn(GT[:], GT[:], ACT.Ln).then_inc(gate("log", 0)[0], 1)
                if t == 27:
                    act.wait_ge(*gate("sums", l))
                    fn(GT[64:96], GU[64:96], ACT.Exp).then_inc(gate("gamma", 0)[0], 1)
                    act.wait_ge(*gate("kd_log", l))
                    fn(ROWB[64:96], ROWB[64:96], ACT.Exp, scale=-1.0).then_inc(gate("kd_exp", 0)[0], 1)
                if t == 29:
                    act.wait_ge(*gate("m", l))
                    fn(EM[:], MC, ACT.Exp, scale=-1.0).then_inc(gate("em", 0)[0], 1)
                    act.wait_ge(*gate("wl_log", l))
                    fn(ROWA[32:32 + H_A], ROWB[0:H_A], ACT.Exp).then_inc(gate("wl_exp", 0)[0], 1)
                    act.wait_ge(*gate("inter_log", l))
                    fn(IR[:, SEQ:T], IR[:, SEQ:T], ACT.Exp).then_inc(gate("inter", 0)[0], 1)

            def store_prompt_state(n):
                act.wait_ge(sem("state_kept"), n + 1)
                act.dma_start(d["sout"][bass.ds(n, 1), :, 0:HD].rearrange("a p e -> p (a e)"), SOUT[:]).then_inc(sem("prompt_out"), 16)

            def gate_exp(n, par):
                act.wait_ge(sem("z_ready"), 4 * n + 4)
                fn(GATE[:], Z[par][:, 3], ACT.Exp, scale=-1.0).then_inc(sem("gate_exp"), 1)

            def gate_log(n):
                act.wait_ge(sem("gate_sum"), n + 1)
                fn(LG[:], GATE[:], ACT.Ln).then_inc(sem("gate_log"), 1)

            def head_scale(n):
                act.wait_ge(sem("head_sums"), n + 1)
                fn(SQH[:], PD[:, 0:T], ACT.Ln, scale=1.0 / HD, bias=EPSC[:, 0:1]).then_inc(sem("head_log"), 1)
                act.wait_ge(sem("scale_log"), n + 1)
                fn(GATE[:], LG[:], ACT.Exp, scale=-1.0).then_inc(sem("head_scale"), 1)

            def linear_head(t, kind, x):
                n, nk, hk, par, pair = x
                mls = kind == "mls"
                if t == 0:
                    gate_exp(n, par)
                if t == 1:
                    gate_log(n)
                    if mls:
                        act.wait_ge(sem("mls_logw"), 4 * (nk + 1))
                        fn(LW[:, 0:384], LW[:, 0:384], ACT.Exp).then_inc(sem("mls_w"), 1)
                        fn(LW[0:NS, 384:416], LW[0:NS, 384:416], ACT.Exp).then_inc(sem("mls_w"), 1)
                if t == 2:
                    act.wait_ge(sem("kv_turned"), n + 1)
                    cols = CUR[:, :, 1] if mls else AUX[par][:, AUX_TAP:AUX_TAP + 3]
                    if mls:
                        act.wait_ge(sem("mls_cur"), 2 * (nk + 1))
                    else:
                        act.wait_ge(sem(f"aux_in{par}"), aux_count(kind, x))
                    fn(U_[:, 0:2].rearrange("p a b -> p (a b)"), PB[:, 0:SEQ]).then_inc(sem(f"{kind}_kept"), 1)
                    for j, (a, b, m) in enumerate(TILES):
                        fn(KW[0:m, j], PA[0:m, j * HD:(j + 1) * HD], scale=cols[0:m, j:j + 1]).then_inc(sem(f"{kind}_kept"), 1)
                    fn(U_[0:NS, 2], PB[0:NS, SEQ:SEQ + HD]).then_inc(sem(f"{kind}_kept"), 1)
                    act.wait_ge(sem(f"{kind}_kept"), 5 * (nk + 1))
                    act.sem_inc(sem("sample_values"), 1)
                if t == 3:
                    act.wait_ge(sem("prompt_state"), n + 1)
                    act.wait_ge(sem("prompt_out"), 16 * (n + 1))
                    fn(SOUT[:], PD[:, 0:HD]).then_inc(sem("state_kept"), 1)
                if t == 4 and mls:
                    act.wait_ge(sem("mls_nout"), 3 * (nk + 1))
                    act.dma_start(d["nout"][bass.ds(nk, 1)].rearrange("a p b -> p (a b)"), NOUT[:]).then_inc(sem("norm_out"), 16)
                if t == 5:
                    store_prompt_state(n)
                    act.wait_ge(sem(f"{kind}_head"), nk + 1)
                    fn(SQH[:], HHD[:], ACT.Square).then_inc(sem("head_squares"), 1)
                if t == 8:
                    head_scale(n)

            def gdn_head(t, x):
                n, nk, hk, par, pair = x
                z = Z[par]
                if t == 0:
                    act.wait_ge(sem("z_ready"), 4 * n + 4)
                    act.wait_ge(sem(f"aux_in{par}"), aux_count("gdn", x))
                    fn(CB[:, :, CONVW - 1:CB_P], z[:, 0:3, 0:SEQ]).then_inc(sem("gdn_conv_in"), 1)
                    cs = CB[:, :, CB_P:CB_N].rearrange("p c (b w) -> p c b w", b=NB)
                    st = AUX[par][:, AUX_STATE:AUX_STATE + CONVS].rearrange("p (c b w) -> p c b w", c=3, b=NB)
                    fn(CB[:, :, 0:CONVW - 1], ONES[:, 0:3].unsqueeze(1).to_broadcast([128, 3, 3]), scale=0.0)\
                        .then_inc(sem("gdn_conv_in"), 1)
                    for c in range(3):
                        fn(cs[:, c, :, CONVW - 1:], z[:, c, SEQ:T].rearrange("p (b t) -> p b t", b=NB)).then_inc(sem("gdn_conv_in"), 1)
                        fn(cs[:, c, :, 0:CONVW - 1], st[:, c]).then_inc(sem("gdn_conv_in"), 1)
                    gate_exp(n, par)
                if t == 1:
                    gate_log(n)
                    act.wait_ge(sem("cnew_out"), 16 * (nk + 1))
                    act.wait_ge(sem("gdn_conv_in"), 8 * (nk + 1))
                    fn(CNEW[:, :, 0:3], CB[:, :, SEQ:SEQ + 3]).then_inc(sem("cnew_ready"), 1)
                    cs = CB[:, :, CB_P:CB_N].rearrange("p c (b w) -> p c b w", b=NB)
                    for c in range(3):
                        fn(CNEW[:, c, 3:].rearrange("p (b w) -> p b w", b=NB), cs[:, c, :, DS:]).then_inc(sem("cnew_ready"), 1)
                if t == 2:
                    act.wait_ge(sem("cnew_ready"), 4 * (nk + 1))
                    act.dma_start(d["cnew"][bass.ds(nk, 1)].rearrange("a p w -> p (a w)"),
                                  CNEW[:].rearrange("p c w -> p (c w)")).then_inc(sem("cnew_out"), 16)
                if t == 3:
                    act.wait_ge(sem(f"bc_in{par}"), aux_count("gdn", x))
                    act.wait_ge(sem("gdn_taps"), 12 * (nk + 1))
                    fn(EE[:], ACC[:], ACT.Exp, scale=-1.0).then_inc(sem("gdn_silu_exp"), 1)
                if t == 4:
                    act.wait_ge(sem("gdn_silu_sum"), nk + 1)
                    fn(EE[:], EE[:], ACT.Ln).then_inc(sem("gdn_silu_log"), 1)
                    act.wait_ge(sem("gdn_silu_log"), nk + 1)
                    fn(EE[:], EE[:], ACT.Exp, scale=-1.0).then_inc(sem("gdn_sigmoid"), 1)
                if t == 5:
                    act.wait_ge(sem("gdn_qkv"), 2 * (nk + 1))
                    fn(EE[:, 0:2, 0:T], z[:, 0:2], ACT.Square).then_inc(sem("gdn_squares"), 1)
                    act.wait_ge(sem("gdn_dx"), 3 * (nk + 1))
                    fn(DX, DX, ACT.Exp, scale=-1.0).then_inc(sem("gdn_decay"), 1)
                    act.wait_ge(sem("gdn_dx2"), 3 * (nk + 1))
                    fn(SC[:, 0:T], SC[:, 0:T], ACT.Exp).then_inc(sem("gdn_decay2"), 1)
                if t == 6:
                    act.wait_ge(sem("gdn_sums"), nk + 1)
                    fn(EE[:, 0:2, 0:T], PCD[:, :, 0:T], ACT.Ln, bias=EPSC[:, 0:1]).then_inc(sem("gdn_l2_log"), 1)
                    act.wait_ge(sem("gdn_l2_log"), nk + 1)
                    fn(EE[:, 0:2, 0:T], EE[:, 0:2, 0:T], ACT.Exp, scale=-0.5).then_inc(sem("gdn_l2"), 1)
                if t == 8:
                    act.wait_ge(sem("kv_turned"), n + 1)
                    act.wait_ge(sem("gdn_cur"), 3 * (nk + 1))
                    for j, (a, b, m) in enumerate(TILES):
                        fn(KW[0:m, j], PA[0:m, j * HD:(j + 1) * HD], scale=CUR[0:m, j, 2:3]).then_inc(sem("gdn_kept"), 1)
                        fn(V_[0:m, j], PB[0:m, j * HD:(j + 1) * HD], scale=CUR[0:m, j, 1:2]).then_inc(sem("gdn_kept"), 1)
                if t == 23:
                    act.wait_ge(sem("gdn_u0"), nk + 1)
                    fn(U_[:, 0], PA[:, 0:HD]).then_inc(sem("gdn_u0_kept"), 1)
                    act.wait_ge(sem("state_read"), n + 1)
                    fn(SMALL[:, 0], PF[:, T:T + NS]).then_inc(sem("gdn_ks_kept"), 1)
                if t == 24:
                    act.wait_ge(sem("gdn_s1"), nk + 1)
                    fn(S1[:], PB[:, 0:HD]).then_inc(sem("gdn_s1_kept"), 1)
                if t == 25:
                    act.wait_ge(sem("gdn_us"), nk + 1)
                    fn(U_[0:NS, 2], PC[0:NS, HD:2 * HD], scale=-1.0).then_inc(sem("sample_values"), 1)
                if t == 26:
                    act.wait_ge(sem("gdn_u1"), nk + 1)
                    fn(U_[:, 1], PA[:, HD:2 * HD], scale=-1.0).then_inc(sem("gdn_u1_kept"), 1)
                if t == 28:
                    store_prompt_state(n)
                    act.wait_ge(sem("gdn_head"), nk + 1)
                    fn(SQH[:], HHD[:], ACT.Square).then_inc(sem("head_squares"), 1)
                if t == 29:
                    head_scale(n)

            def mixer(t, kind, l, x):
                if kind == "gdn":
                    gdn_head(t, x)
                elif kind in ("ret", "mls"):
                    linear_head(t, kind, x)
                elif kind == "first":
                    gates(t, l)

            def quad(Q, kind, l, x):
                for t in range(SLOTS):
                    mixer(t, kind, l, x)
                    s, c = divmod(t, 8)
                    if kind == "up" and c == 7:
                        act.wait_ge(sem("up_relu"), up_units(l, x, s) + 1)
                        fn(UPT[s % 2], UPE[s % 2], ACT.Square).then_inc(sem("up_square"), 1)
                    if t % 2:
                        hi_part(Q, (t + 1) // 2 + 4)

            def mix_alone(kind, l, x):
                for t in range(SLOTS):
                    mixer(t, kind, l, x)

            def after_out(l):
                act.wait_ge(sem("y_ready"), (2 * l + 1) * NC_)
                squares(4 * l + 1, Y)
                norm_scale(4 * l + 1, RS, "rs_ready")
                prenorm(l, 2, 2)

            def after_mlp(l):
                act.wait_ge(sem("y_ready"), (2 * l + 2) * NC_)
                squares(4 * l + 3, Y)
                norm_scale(4 * l + 3, RS, "rs_ready")

            act.wait_ge(sem("ones_set"), 1)
            for p in range(5):
                hi_part(0, p)
            walk(act, lambda l: prenorm(l, 0, 0), quad, mix_alone, after_out, after_mlp)
            act.wait_ge(sem("cnew_out"), 16 * (DEPTH * H_C + 1))
            act.wait_ge(sem("norm_out"), 16 * (DEPTH * H_A + 1))
            act.wait_ge(sem("prompt_out"), 16 * (DEPTH * HEADS + 1))

        @block.vector
        def _(dve):
            tt, ts, stt = nc.vector.tensor_tensor, nc.vector.tensor_scalar, nc.vector.scalar_tensor_tensor

            def lo_part(Q, p):
                s, c = divmod(p, 4)
                if c == 0:
                    dve.wait_ge(sem("unit_done"), 4 * Q + s + 1)
                dve.wait_ge(sem("hi_ready"), 16 * Q + p + 1)
                k = slice(4 * c, 4 * c + 4)
                tt(WL[s % 2][:, k], RAW[c][:], WH[s % 2][:, k].bitcast(F32), ALU.subtract).then_inc(sem("lo_ready"), 1)

            def prenorm_lo(l, which, gain):
                for c in range(NC_):
                    dve.wait_ge(sem("hh_ready"), (2 * l + which) * NC_ + c + 1)
                    stt(HL[:, c], X[:, c], NG[:, gain, c:c + 1], HH[:, c].bitcast(F32), ALU.mult, ALU.subtract)\
                        .then_inc(sem("hl_ready"), 1)

            def update_x(l, which, gain):
                e = 2 * l + which
                dve.wait_ge(sem("rs_ready"), e + 1)
                for g in range(4):
                    for c in range(4 * g, 4 * g + 4):
                        stt(Y[:, c], Y[:, c], NG[:, gain, c:c + 1], RS[:], ALU.mult, ALU.mult).then_inc(sem("y_scaled"), 1)
                    dve.wait_ge(sem("y_scaled"), NC_ * e + 4 * g + 4)
                    k = slice(4 * g, 4 * g + 4)
                    tt(X[:, k], X[:, k], Y[:, k], ALU.add).then_inc(sem("x_updated"), 1)
                dve.wait_ge(sem("x_updated"), 4 * (e + 1))

            def gates(t, l):
                if t == 0:
                    dve.wait_ge(sem("gate_in"), 16 * 4 * (l + 1))
                    dve.wait_ge(sem("gains_in"), 16 * (l + 1))
                    tt(GWf, GWf, NG[:, 0].unsqueeze(2).to_broadcast([128, NC_, HD]), ALU.mult).then_inc(gate("weights", 0)[0], 1)
                if t == 23:
                    dve.wait_ge(sem("s_ready"), 2 * l + 1)
                    dve.wait_ge(*gate("proj", l))
                    tt(ZG, PD[:, 0:T], S[:], ALU.mult).then_inc(gate("z", 0)[0], 1)
                    dve.wait_ge(*gate("z", l))
                    ts(ZG, ZG, GP[:, 0:1], None, ALU.add).then_inc(gate("biased", 0)[0], 1)
                if t == 24:
                    dve.wait_ge(*gate("tanh_exp", l))
                    ts(GE[0:64], GE[0:64], 1.0, None, ALU.add).then_inc(gate("tanh_sum", 0)[0], 1)
                    dve.wait_ge(*gate("tanh_sum", l))
                    nc.vector.reciprocal(GE[0:64], GE[0:64]).then_inc(gate("tanh_rec", 0)[0], 1)
                    dve.wait_ge(*gate("tanh_rec", l))
                    ts(GU[0:64], GE[0:64], -2.0 * SOFTCAP, SOFTCAP, ALU.mult, ALU.add).then_inc(gate("capped", 0)[0], 1)
                    dve.wait_ge(*gate("beta_exp", l))
                    ts(ROWA[96:128], ROWA[96:128], 1.0, None, ALU.add).then_inc(gate("beta_sum", 0)[0], 1)
                    dve.wait_ge(*gate("beta_sum", l))
                    nc.vector.reciprocal(ROWA[96:128], ROWA[96:128]).then_inc(gate("beta", 0)[0], 1)
                    dve.wait_ge(*gate("capped", l))
                    ts(ZG[0:64], GU[0:64], -1.0, None, ALU.mult).then_inc(gate("y", 0)[0], 1)
                    dve.wait_ge(*gate("y", l))
                    stt(GE, ZG, -1.0, ZG, ALU.mult, ALU.max).then_inc(gate("abs", 0)[0], 1)
                if t == 25:
                    dve.wait_ge(*gate("sp_exp", l))
                    ts(GT, GE, 1.0, None, ALU.add).then_inc(gate("u", 0)[0], 1)
                    dve.wait_ge(*gate("u", l))
                    stt(SQH[:], GT, -1.0, GE, ALU.add, ALU.subtract).then_inc(gate("rest", 0)[0], 1)
                    dve.wait_ge(*gate("log", l))
                    dve.wait_ge(*gate("rest", l))
                    tt(GT, GT, SQH[:], ALU.subtract).then_inc(gate("log1p", 0)[0], 1)
                    dve.wait_ge(*gate("log1p", l))
                    stt(GT, ZG, 0.0, GT, ALU.max, ALU.add).then_inc(gate("softplus", 0)[0], 1)
                    dve.wait_ge(*gate("softplus", l))
                    dve.wait_ge(*gate("rate", l))
                    ts(GT, GT, GP[:, 1:2], -1.0, ALU.mult, ALU.mult).then_inc(gate("decay", 0)[0], 1)
                if t == 26:
                    ts(EXTI[:, 1:EXT_P], GU[0:H_A, 0:SEQ], 1.0, None, ALU.mult).then_inc(gate("ext", 0)[0], 1)
                    ei = EXTI[:, EXT_P:EXT].rearrange("p (b t) -> p b t", b=NB)
                    ef = EXTF[:, EXT_P:EXT].rearrange("p (b t) -> p b t", b=NB)
                    ts(ei[:, :, 1:], sview(GU[0:H_A]), 1.0, None, ALU.mult).then_inc(gate("ext", 0)[0], 1)
                    ts(ei[:, :, 0:1], MI[:].unsqueeze(2), 1.0, None, ALU.mult).then_inc(gate("ext", 0)[0], 1)
                    nc.vector.memset(EXTI[:, 0:1], 0.0).then_inc(gate("ext", 0)[0], 1)
                    nc.vector.memset(EXTF, BIG).then_inc(gate("ext_f", 0)[0], 1)
                    dve.wait_ge(*gate("decay", l))
                    dve.wait_ge(*gate("ext_f", l))
                    ts(EXTF[:, 1:EXT_P], GT[32:32 + H_A, 0:SEQ], 1.0, None, ALU.mult).then_inc(gate("ext", 0)[0], 1)
                    ts(ef[:, :, 1:], sview(GT[32:32 + H_A]), 1.0, None, ALU.mult).then_inc(gate("ext", 0)[0], 1)
                    dve.wait_ge(*gate("ext", l))
                    nc.vector.tensor_tensor_scan(SQH[:], RESETS, GT, 0.0, ALU.mult, ALU.add).then_inc(gate("scan", 0)[0], 1)
                    nc.vector.tensor_tensor_scan(EXTM, EXTF, EXTI, 0.0, ALU.add, ALU.max).then_inc(gate("scan", 0)[0], 1)
                    dve.wait_ge(*gate("scan", l))
                    ts(LG[0:H_A], GU[0:H_A], 1.0, None, ALU.mult).then_inc(gate("i", 0)[0], 1)
                    ts(F0, SQH[32:32 + H_A], 1.0, None, ALU.mult).then_inc(gate("f", 0)[0], 1)
                    ts(MC[:, 0:SEQ], EXTM[:, 1:EXT_P], 1.0, None, ALU.mult).then_inc(gate("m", 0)[0], 1)
                    em = EXTM[:, EXT_P:EXT].rearrange("p (b t) -> p b t", b=NB)
                    ts(sview(MC), em[:, :, 1:], 1.0, None, ALU.mult).then_inc(gate("m", 0)[0], 1)
                    dve.wait_ge(*gate("i", l))
                    ts(GU[64:96], SQH[64:96], 1.0, None, ALU.mult).then_inc(gate("sums", 0)[0], 1)
                    ts(MOUT[:, 0:1], EXTM[:, SEQ:SEQ + 1], 1.0, None, ALU.mult).then_inc(gate("mout", 0)[0], 1)
                    ts(MOUT[:, 1:].unsqueeze(2), em[:, :, DS:DS + 1], 1.0, None, ALU.mult).then_inc(gate("mout", 0)[0], 1)
                if t == 27:
                    ts(ROWA[64:96], SQH[64:96], 1.0, None, ALU.mult).then_inc(gate("rows", 0)[0], 1)
                    dve.wait_ge(*gate("sums", l))
                    for a, b in ((0, HD), (HD, SEQ)):
                        ts(ROWB[64:96, a:b], GU[64:96, a:b], GU[64:96, b - 1:b], None, ALU.subtract).then_inc(gate("kd_log", 0)[0], 1)
                    gu = sview(GU[64:96])
                    tt(sview(ROWB[64:96]), gu, gu[:, :, DS - 1:DS].to_broadcast([32, NB, DS]), ALU.subtract).then_inc(gate("kd_log", 0)[0], 1)
                    dve.wait_ge(*gate("m", l))
                    dve.wait_ge(*gate("f", l))
                    tt(AR[:], F0, MC, ALU.subtract).then_inc(gate("a", 0)[0], 1)
                    tt(ROWA[0:H_A], LG[0:H_A], F0, ALU.subtract).then_inc(gate("b", 0)[0], 1)
                    dve.wait_ge(*gate("a", l))
                    dve.wait_ge(*gate("b", l))
                    ts(ROWB[0:H_A, 0:SEQ], ROWA[0:H_A, 0:SEQ], AR[:, SEQ - 1:SEQ], None, ALU.add).then_inc(gate("wl_log", 0)[0], 1)
                    ar = sview(AR)
                    tt(sview(ROWB[0:H_A]), sview(ROWA[0:H_A]), ar[:, :, DS - 1:DS].to_broadcast([H_A, NB, DS]), ALU.add)\
                        .then_inc(gate("wl_log", 0)[0], 1)
                    tt(sview(IR), ar, MI[:].unsqueeze(2).to_broadcast([H_A, NB, DS]), ALU.add).then_inc(gate("inter_log", 0)[0], 1)
                if t == 30:
                    dve.wait_ge(*gate("wl_exp", l))
                    ts(ROWA[32:32 + H_A], ROWA[32:32 + H_A], SCALE, None, ALU.mult).then_inc(gate("wl", 0)[0], 1)
                if t == 31:
                    dve.wait_ge(*gate("turned", l))
                    for dst, src in ((COLA, PE_), (COLB, PF)):
                        nc.vector.tensor_copy(dst[:, 0:2].rearrange("p a b -> p (a b)"), src[:, 0:SEQ]).then_inc(gate("cols", 0)[0], 1)
                        nc.vector.tensor_copy(dst[0:NS, 2], src[0:NS, SEQ:SEQ + HD]).then_inc(gate("cols", 0)[0], 1)

            def cap_gate(n):
                dve.wait_ge(sem("gate_exp"), n + 1)
                ts(GATE[:], GATE[:], CAP, 1.0, ALU.min, ALU.add).then_inc(sem("gate_sum"), 1)

            def finish(n, par, silu):
                dve.wait_ge(sem("head_log"), n + 1)
                dve.wait_ge(sem("gate_log"), n + 1)
                stt(LG[:], SQH[:], 0.5, LG[:], ALU.mult, ALU.add).then_inc(sem("scale_log"), 1)
                dve.wait_ge(sem("head_scale"), n + 1)
                stt(YY[:], HHD[:], AUX[par][:, AUX_GAIN:AUX_GAIN + 1], GATE[:], ALU.mult, ALU.mult).then_inc(sem("y_head"), 1)
                dve.wait_ge(sem("y_head"), n + 1)
                y = YY
                if silu:
                    tt(HHD[:], YY[:], Z[par][:, 3], ALU.mult).then_inc(sem("y_gated"), 1)
                    y = HHD
                return y

            def store_u(n, l, c, y):
                ts(UH[:, c].rearrange("p a t -> p (a t)"), y[:], 1.0, None, ALU.mult).then_inc(sem("uh_head"), 1)
                dve.wait_ge(sem("uh_head"), n + 1)
                tt(UL[:, c].rearrange("p a t -> p (a t)"), y[:], UH[:, c].rearrange("p a t -> p (a t)").bitcast(F32), ALU.subtract)\
                    .then_inc(sem("ul_ready"), 1)
                dve.wait_ge(sem("ul_ready"), l * (NC_ * MLP_Q) + n + 1)
                dve.sem_inc(sem("head_done"), 1)

            def add_state(n):
                dve.wait_ge(sem("sample_state"), n + 1)
                dve.wait_ge(sem("state_decayed"), n + 1)
                dve.wait_ge(sem("state_kept"), n + 1)
                tt(CDEC.rearrange("p b e -> p (b e)"), CDEC.rearrange("p b e -> p (b e)"),
                   PAB[:].rearrange("p a b -> p (a b)"), ALU.add).then_inc(sem("state_ready"), 1)

            def chunk_of(kind, hk):
                base = {"gdn": 0, "ret": H_C, "mls": H_C + H_B}[kind]
                return bass.ds(base + hk, 1)

            def linear_head(t, kind, l, x):
                n, nk, hk, par, pair = x
                mls = kind == "mls"
                z, bc, aux = Z[par], BC[par], AUX[par]
                if t == 0:
                    cap_gate(n)
                    dve.wait_ge(sem(f"aux_in{par}"), aux_count(kind, x))
                    if mls:
                        for j, r in ((0, 0), (1, 32)):
                            if j == 0:
                                dve.wait_ge(*gate("cols", l))
                            ts(CUR[:, :, j:j + 1], COLA[:, :, bass.ds(hk + r, 1)], 1.0, None, ALU.mult).then_inc(sem("mls_cur"), 1)
                    else:
                        tt(ACC[:, 0:2, 0:T], z[:, 0:2], con["c_cos"][:].unsqueeze(1).to_broadcast([128, 2, T]), ALU.mult)\
                            .then_inc(sem("ret_qk"), 1)
                        dve.wait_ge(sem("ret_rotated"), nk + 1)
                        tt(EE[:, 0:2, 0:T], PCD[:, :, 0:T], con["c_sin"][:].unsqueeze(1).to_broadcast([128, 2, T]), ALU.mult)\
                            .then_inc(sem("ret_qk"), 1)
                        dve.wait_ge(sem("ret_qk"), 3 * nk + 2)
                        tt(QK2, ACC[:, 0:2, 0:T], EE[:, 0:2, 0:T], ALU.add).then_inc(sem("ret_qk"), 1)
                if t == 1 and mls:
                    dve.wait_ge(sem("mls_cur"), 2 * (nk + 1))
                    dve.wait_ge(sem(f"bc_in{par}"), aux_count(kind, x))
                    never = con["c_never"]
                    stt(LW[:, 0:HD], bc[:, 0:HD], CUR[:, 0, 0:1], never[:], ALU.add, ALU.add).then_inc(sem("mls_logw"), 1)
                    ts(LW[:, HD:SEQ], bc[:, HD:SEQ], CUR[:, 0, 0:1], None, ALU.add).then_inc(sem("mls_logw"), 1)
                    stt(LW[:, SEQ:384], bc[:, HD:SEQ], CUR[:, 1, 0:1], never[:], ALU.add, ALU.add).then_inc(sem("mls_logw"), 1)
                    stt(LW[0:NS, 384:416], bc[0:NS, SEQ:T], CUR[0:NS, 2, 0:1], con["c_never_s"][0:NS], ALU.add, ALU.add)\
                        .then_inc(sem("mls_logw"), 1)
                if t == 2:
                    q = z[:, 0] if mls else QK2[:, 0]
                    if not mls:
                        dve.wait_ge(sem("ret_qk"), 3 * (nk + 1))
                        dve.wait_ge(sem(f"bc_in{par}"), aux_count(kind, x))
                    tt(SMALL[:, 0], q[:, SEQ:T], bc[:, 2 * T:], ALU.mult).then_inc(sem(f"{kind}_qs"), 1)
                    dve.wait_ge(sem("scores"), n + 1)
                    if mls:
                        dve.wait_ge(sem("mls_w"), 2 * (nk + 1))
                        stt(SC[:, 0:384], PE_[:, 0:384], SCALE, LW[:, 0:384], ALU.mult, ALU.mult).then_inc(sem("mls_probs"), 1)
                        stt(SC[0:NS, 384:416], PE_[0:NS, 384:416], SCALE, LW[0:NS, 384:416], ALU.mult, ALU.mult)\
                            .then_inc(sem("mls_probs"), 1)
                        dve.wait_ge(sem("mls_qs"), nk + 1)
                        nin = aux[:, AUX_STATE:AUX_STATE + NB].unsqueeze(2).to_broadcast([128, NB, DS])
                        tt(SMALL[:, 1].rearrange("p (b t) -> p b t", b=NB), SMALL[:, 0].rearrange("p (b t) -> p b t", b=NB),
                           nin, ALU.mult).then_inc(sem("mls_qn"), 1)
                    else:
                        dm = aux[:, AUX_STATE:AUX_STATE + T]
                        stt(SC[:, 0:SEQ], PE_[:, 0:SEQ], SCALE, dm[:, 0:SEQ], ALU.mult, ALU.mult).then_inc(sem("ret_probs"), 1)
                        stt(SC[:, SEQ:384], PE_[:, SEQ:384], SCALE, dm[:, 0:HD], ALU.mult, ALU.mult).then_inc(sem("ret_probs"), 1)
                        stt(SC[0:NS, 384:416], PE_[0:NS, 384:416], SCALE, dm[0:NS, SEQ:T], ALU.mult, ALU.mult)\
                            .then_inc(sem("ret_probs"), 1)
                if t == 3:
                    dve.wait_ge(sem(f"{kind}_out"), nk + 1)
                    if mls:
                        stt(YY[:], PC[:, 0:T], -1.0, bc[:, T:2 * T], ALU.mult, ALU.max).then_inc(sem("mls_den"), 1)
                        dve.wait_ge(sem("mls_den"), 3 * nk + 1)
                        tt(YY[:], PC[:, 0:T], YY[:], ALU.max).then_inc(sem("mls_den"), 1)
                        dve.wait_ge(sem("mls_den"), 3 * nk + 2)
                        nc.vector.reciprocal(YY[:], YY[:]).then_inc(sem("mls_den"), 1)
                        dve.wait_ge(sem("mls_den"), 3 * nk + 3)
                        tt(HHD[:], PF[:, 0:T], YY[:], ALU.mult).then_inc(sem("mls_head"), 1)
                        dve.wait_ge(sem("prompt_state"), n + 1)
                        dve.wait_ge(sem("norm_out"), 16 * (nk + 1))
                        tt(NOUT[:, 1:], aux[:, AUX_STATE:AUX_STATE + NB], bc[:, 2 * T + DS - 1:BCW:DS], ALU.mult)\
                            .then_inc(sem("mls_nout"), 1)
                        dve.wait_ge(sem("mls_nout"), 3 * nk + 1)
                        dve.wait_ge(sem("state_kept"), n + 1)
                        tt(NOUT[:, 1:], NOUT[:, 1:], PD[:, HD + 1:HD + 1 + NB], ALU.add).then_inc(sem("mls_nout"), 1)
                        nc.vector.tensor_copy(NOUT[:, 0:1], PD[:, HD:HD + 1]).then_inc(sem("mls_nout"), 1)
                    else:
                        nc.vector.tensor_copy(YY[:], PF[:, 0:T]).then_inc(sem("ret_kept_out"), 1)
                if t == 4 and not mls:
                    dve.wait_ge(sem("ret_centered"), nk + 1)
                    nc.vector.tensor_copy(HHD[:], PC[:, 0:T]).then_inc(sem("ret_head"), 1)
                if t == 8:
                    y = finish(n, par, not mls)
                    if not mls:
                        dve.wait_ge(sem("y_gated"), silu_count(l, kind, hk))
                    store_u(n, l, chunk_of(kind, hk), y)
                if t == 10:
                    add_state(n)

            def silu_count(l, kind, hk):
                return l * (H_C + H_B) + (H_C if kind == "ret" else 0) + hk + 1

            def gdn_head(t, l, x):
                n, nk, hk, par, pair = x
                bc, aux, U3 = BC[par], AUX[par], Z[par][:, 0:3]
                if t == 0:
                    cap_gate(n)
                    dve.wait_ge(*gate("cols", l))
                    for j, (src, r) in enumerate(((COLA, 64), (COLA, 96), (COLB, 64))):
                        ts(CUR[:, :, j:j + 1], src[:, :, bass.ds(hk + r, 1)], 1.0, None, ALU.mult).then_inc(sem("gdn_cur"), 1)
                    dve.wait_ge(sem("gdn_conv_in"), 8 * (nk + 1))
                if t in (0, 1, 2):
                    c = t
                    for w in range(CONVW):
                        tap = aux[:, AUX_TAP + 4 * c + w:AUX_TAP + 4 * c + w + 1]
                        if w == 0:
                            ts(ACC[:, c], CB[:, c, w:w + CO], tap, None, ALU.mult).then_inc(sem("gdn_taps"), 1)
                        else:
                            dve.wait_ge(sem("gdn_taps"), 12 * nk + 4 * c + w)
                            stt(ACC[:, c], CB[:, c, w:w + CO], tap, ACC[:, c], ALU.mult, ALU.add).then_inc(sem("gdn_taps"), 1)
                if t == 3:
                    dve.wait_ge(sem("gdn_silu_exp"), nk + 1)
                    ts(EE[:], EE[:], CAP, 1.0, ALU.min, ALU.add).then_inc(sem("gdn_silu_sum"), 1)
                    dve.wait_ge(sem(f"bc_in{par}"), aux_count("gdn", x))
                    dve.wait_ge(sem("gdn_cur"), 3 * (nk + 1))
                    for j, (a, b, m) in enumerate(TILES):
                        ts(DX[:, a:b], bc[:, a:b], CUR[:, j, 0:1], 0.0, ALU.subtract, ALU.max).then_inc(sem("gdn_dx"), 1)
                    for j, (a, b, m) in enumerate(TILES):
                        ts(SC[:, a:b], bc[:, a:b], CUR[:, j, 0:1], 0.0, ALU.subtract, ALU.min).then_inc(sem("gdn_dx2"), 1)
                if t == 4:
                    dve.wait_ge(sem("gdn_sigmoid"), nk + 1)
                    tt(U3[:, :, 0:SEQ], ACC[:, :, 0:SEQ], EE[:, :, 0:SEQ], ALU.mult).then_inc(sem("gdn_qkv"), 1)
                    w = CONVW - 1 + DS
                    acc_s, ee_s = [bass_strided(a, w) for a in (ACC, EE)]
                    tt(U3[:, :, SEQ:T].rearrange("p c (b t) -> p c b t", b=NB), acc_s, ee_s, ALU.mult).then_inc(sem("gdn_qkv"), 1)
                if t == 6:
                    dve.wait_ge(sem("gdn_l2"), nk + 1)
                    tt(QK2, U3[:, 0:2], EE[:, 0:2, 0:T], ALU.mult).then_inc(sem("gdn_qk"), 1)
                    dve.wait_ge(sem("gdn_qk"), nk + 1)
                    stt(QKG[:, 0], QK2[:, 0], SCALE, bc[:, T:2 * T], ALU.mult, ALU.mult).then_inc(sem("gdn_qkg"), 1)
                    tt(QKG[:, 1], QK2[:, 1], bc[:, T:2 * T], ALU.mult).then_inc(sem("gdn_qkg"), 1)
                if t == 8:
                    dve.wait_ge(sem("gdn_kk"), nk + 1)
                    dve.wait_ge(sem("gdn_decay"), nk + 1)
                    for j, (a, b, m) in enumerate(TILES):
                        stt(AM[0:m, a:b], PC[0:m, a:b], CUR[0:m, j, 1:2], DX[0:m, a:b], ALU.mult, ALU.mult).then_inc(sem("gdn_A"), 1)
                    dve.wait_ge(sem("scores"), n + 1)
                    dve.wait_ge(sem("gdn_decay2"), nk + 1)
                    stt(SC[:, 0:SEQ], PF[:, 0:SEQ], SCALE, SC[:, 0:SEQ], ALU.mult, ALU.mult).then_inc(sem("gdn_scores"), 1)
                    stt(SC[0:NS, SEQ:T], PF[0:NS, SEQ:T], SCALE, SC[0:NS, SEQ:T], ALU.mult, ALU.mult).then_inc(sem("gdn_scores"), 1)
                if t == 9:
                    dve.wait_ge(sem("gdn_scores"), 2 * (nk + 1))
                    sc = SC[:, 0:SEQ].rearrange("p (a b) -> p a b", a=2)
                    tt(sc, sc, con["c_causal"][:].unsqueeze(1).to_broadcast([128, 2, HD]), ALU.mult).then_inc(sem("gdn_probs"), 1)
                    tt(SC[0:NS, SEQ:T], SC[0:NS, SEQ:T], con["c_causal_s"][0:NS], ALU.mult).then_inc(sem("gdn_probs"), 1)
                if 9 <= t < 9 + 2 * LEVELS:
                    lev, second = divmod(t - 9, 2)
                    mask = con["c_levels"]
                    if not second:
                        dve.wait_ge(sem("gdn_P"), LEVELS * nk + lev + 1)
                        if lev < 2:
                            tt(PM[0:NS, SEQ:T], PD[0:NS, SEQ:T], mask[0:NS, lev, 0:NS], ALU.mult).then_inc(sem("gdn_Pm_s"), 1)
                        tt(PM[:, 0:SEQ].rearrange("p (a b) -> p a b", a=2), PD[:, 0:SEQ].rearrange("p (a b) -> p a b", a=2),
                           mask[:, lev].unsqueeze(1).to_broadcast([128, 2, HD]), ALU.mult).then_inc(sem("gdn_Pm"), 1)
                    else:
                        dve.wait_ge(sem("gdn_TR"), LEVELS * nk + lev + 1)
                        pe4 = PE_[:].rearrange("p (a b) -> p a b", a=4)
                        ident = IDENT[:].unsqueeze(1)
                        if lev < 2:
                            old = IDENT[0:NS, 0:NS].unsqueeze(1).to_broadcast([NS, 2, NS]) if lev == 0 else TS[:]
                            if lev:
                                dve.wait_ge(sem("gdn_inverse_s"), 2 * nk + 1)
                            tt(TS[:], old, PC[0:NS, 0:2 * NS].rearrange("p (a b) -> p a b", a=2), ALU.subtract)\
                                .then_inc(sem("gdn_inverse_s"), 1)
                        old = ident.to_broadcast([128, 4, HD]) if lev == 0 else TR
                        if lev:
                            dve.wait_ge(sem("gdn_inverse"), LEVELS * nk + lev)
                        tt(TR, old, pe4, ALU.subtract).then_inc(sem("gdn_inverse"), 1)
                if t == 24:
                    dve.wait_ge(sem("gdn_ks_turned"), nk + 1)
                    dve.wait_ge(sem("gdn_kept"), 6 * (nk + 1))
                    stt(RHS[0:NS, 1], PC[0:NS, 0:HD], CUR[0:NS, 2, 1:2], V_[0:NS, 2], ALU.mult, ALU.subtract).then_inc(sem("gdn_rhs_s"), 1)
                if t == 25:
                    dve.wait_ge(sem("gdn_ks"), nk + 1)
                    stt(RHS[:, 0], PB[:, HD:2 * HD], CUR[:, 1, 1:2], V_[:, 1], ALU.mult, ALU.subtract).then_inc(sem("gdn_rhs"), 1)
                if t == 27:
                    dve.wait_ge(sem("prompt_state"), n + 1)
                    dve.wait_ge(sem("gdn_s1_kept"), nk + 1)
                    dve.wait_ge(sem("prompt_out"), 16 * (n + 1))
                    stt(SOUT[:], S1[:], bc[:, T + SEQ - 1:T + SEQ], PB[:, 2 * HD:3 * HD], ALU.mult, ALU.add).then_inc(sem("state_kept"), 1)
                    dve.wait_ge(sem("gdn_out"), nk + 1)
                    nc.vector.tensor_copy(HHD[:], PF[:, 0:T]).then_inc(sem("gdn_head"), 1)
                if t == 29:
                    y = finish(n, par, True)
                    dve.wait_ge(sem("y_gated"), silu_count(l, "gdn", hk))
                    store_u(n, l, chunk_of("gdn", hk), y)
                if t == 30:
                    add_state(n)

            def bass_strided(a, w):
                whole = a[:, :, CB_P:CO]
                pad = NB * w - (CO - CB_P)
                assert pad == w - DS
                base = a[:, :, CB_P - pad:CO].rearrange("p c (b t) -> p c b t", b=NB)
                return base[:, :, :, pad:]

            def evac(Q, s, kind, l, x):
                dve.wait_ge(sem("unit_done"), 4 * Q + s + 3)
                psum = PU[s % 2][:, 0:T]
                if kind in ("first", "gdn", "ret", "mls"):
                    if kind == "first" and s == 0:
                        dve.wait_ge(sem("s_ready"), 2 * l + 1)
                    par = 0 if kind == "first" else 1 - x[3]
                    i = tt(Z[par][:, s], psum, S[:], ALU.mult)
                    i.then_inc(sem("z_ready"), 1)
                    dve.wait_ge(sem("z_ready"), z_before(Q, kind, l, x) + s + 1)
                elif kind == "up":
                    u = up_units(l, x, s)
                    if s == 0:
                        dve.wait_ge(sem("s_ready"), 2 * l + 2)
                    stt(UPE[s % 2], psum, 0.0, S[:], ALU.max, ALU.mult).then_inc(sem("up_relu"), 1)
                    dve.wait_ge(sem("up_relu"), u + 1)
                elif kind == "out":
                    c = bass.ds(4 * x[1] + s, 1)
                    if s == 0:
                        dve.wait_ge(sem("state_ready"), (l + 1) * HEADS + 1)
                        dve.wait_ge(sem("state_out"), 16 * HEADS * (l + 1))
                    ts(Y[:, c].rearrange("p a t -> p (a t)"), psum, 1.0, None, ALU.mult).then_inc(sem("y_ready"), 1)
                    dve.wait_ge(sem("y_ready"), 2 * l * NC_ + 4 * x[1] + s + 1)
                else:
                    c = bass.ds(4 * x[1] + s, 1)
                    yc = Y[:, c].rearrange("p a t -> p (a t)")
                    if kind == "down0":
                        ts(yc, psum, 1.0, None, ALU.mult).then_inc(sem("y_added"), 1)
                    else:
                        tt(yc, yc, psum, ALU.add).then_inc(sem("y_added"), 1)
                    dve.wait_ge(sem("y_added"), (l * MLP_Q + x[0]) * NC_ + 4 * x[1] + s + 1)
                dve.sem_inc(sem("psum_read"), 1)

            def z_before(Q, kind, l, x):
                return l * (4 * HEADS) if kind == "first" else 4 * (x[0] + 1)

            def store_up(l, x, s):
                u = up_units(l, x, s)
                dve.wait_ge(sem("up_square"), u + 1)
                c = bass.ds(4 * x[1] + s, 1)
                uh = UH[:, c].rearrange("p a t -> p (a t)")
                ts(uh, UPT[s % 2], 1.0, None, ALU.mult).then_inc(sem("uh_ready"), 1)
                dve.wait_ge(sem("uh_ready"), u + 1)
                tt(UL[:, c].rearrange("p a t -> p (a t)"), UPT[s % 2], uh.bitcast(F32), ALU.subtract).then_inc(sem("ul_ready"), 1)

            def mixer(t, kind, l, x):
                if kind == "gdn":
                    gdn_head(t, l, x)
                elif kind in ("ret", "mls"):
                    linear_head(t, kind, l, x)
                elif kind == "first":
                    gates(t, l)

            def quad(Q, kind, l, x):
                for t in range(SLOTS):
                    if t % 2 == 0:
                        lo_part(Q, t // 2 + 4)
                    mixer(t, kind, l, x)
                    if t % 8 == 7:
                        evac(Q, t // 8, kind, l, x)
                        if kind == "up":
                            store_up(l, x, t // 8)

            def mix_alone(kind, l, x):
                for t in range(SLOTS):
                    mixer(t, kind, l, x)

            def after_out(l):
                update_x(l, 0, 1)
                prenorm_lo(l, 1, 2)

            def after_mlp(l):
                dve.wait_ge(sem("y_added"), (l + 1) * MLP_Q * NC_)
                for c in range(NC_):
                    dve.sem_inc(sem("y_ready"), 1)
                update_x(l, 1, 3)
                dve.sem_inc(sem("layer_free"), 1)
                dve.sem_inc(sem("x_final"), 1)

            for a, v in ((ONES, 1.0), (EPSC, EPS), (ROWA, 0.0), (ROWB, 0.0), (CUR, 0.0), (COLA, 0.0), (COLB, 0.0)):
                nc.vector.memset(a[:], v).then_inc(sem("constants_set"), 1)
            dve.wait_ge(sem("constants_set"), 7)
            dve.sem_inc(sem("ones_set"), 1)
            dve.sem_inc(sem("layer_free"), 1)
            dve.sem_inc(sem("state_ready"), 1)
            dve.sem_inc(sem("head_done"), 1)
            dve.wait_ge(sem("constants_in"), 16 * len(con))
            dve.wait_ge(sem("x_in"), 16)
            for p in range(4):
                lo_part(0, p)
            walk(dve, lambda l: prenorm_lo(l, 0, 0), quad, mix_alone, after_out, after_mlp)



def kernel(**inputs):
    import concourse.bacc as _bacc
    from concourse.bass_utils import run_bass_kernel_spmd as _run

    a = {k: np.ascontiguousarray(v) for k, v in inputs.items()}
    D = DEPTH
    w_in = a["w_in"]
    cols_a = [g * H_A * HD for g in range(4)]
    base_b = 4 * H_A * HD + 2 * H_A
    cols_b = [base_b + g * H_B * HD for g in range(4)]
    base_c = base_b + 4 * H_B * HD
    cols_c = [base_c + g * H_C * HD for g in range(4)]
    heads = [(cols_c, h) for h in range(H_C)] + [(cols_b, h) for h in range(H_B)] + [(cols_a, h) for h in range(H_A)]
    rows = [H_A + H_B + h for h in range(H_C)] + [H_A + h for h in range(H_B)] + list(range(H_A))

    w = np.empty((D * QUADS * 4 + 2, 128, NC_, HD), np.float32)
    n = 0
    for l in range(D):
        for cols, h in heads:
            for g in range(4):
                c = cols[g] + h * HD
                w[n] = w_in[l, :, c:c + HD].reshape(NC_, 128, HD).transpose(1, 0, 2)
                n += 1
        w_out = a["w_out"][l].reshape(HEADS, 128, D_MODEL)[rows]
        for j in range(NC_):
            w[n] = w_out[:, :, j * HD:(j + 1) * HD].transpose(1, 0, 2)
            n += 1
        for q in range(MLP_Q):
            for j in range(NC_):
                c = (q * NC_ + j) * HD
                w[n] = a["w_up"][l, :, c:c + HD].reshape(NC_, 128, HD).transpose(1, 0, 2)
                n += 1
            for j in range(NC_):
                part = a["w_down"][l, q * D_MODEL:(q + 1) * D_MODEL, j * HD:(j + 1) * HD]
                w[n] = part.reshape(NC_, 128, HD).transpose(1, 0, 2)
                n += 1
    w[n:] = w[0:2]

    base_g = 4 * H_A * HD
    end_c = base_c + 4 * H_C * HD
    gw = np.zeros((D, 128, NC_, HD), np.float32)
    for to, frm, k in ((0, base_g, H_A), (32, base_g + H_A, H_A), (64, end_c, H_C), (96, end_c + H_C, H_C)):
        gw[..., to:to + k] = w_in[:, :, frm:frm + k].reshape(D, NC_, 128, k).transpose(0, 2, 1, 3)
    gp = np.zeros((D, 128, 2), np.float32)
    gp[:, 0:H_A, 0] = a["mlstm_gate_bias"][:, :H_A]
    gp[:, 32:32 + H_A, 0] = a["mlstm_gate_bias"][:, H_A:]
    gp[:, 64:64 + H_C, 0] = a["gdn_dt_bias"]
    gp[:, 64:64 + H_C, 1] = a["gdn_A_log"]
    ng = np.stack([a[k].reshape(D, NC_, 128).transpose(0, 2, 1)
                   for k in ("norm_mix_pre", "norm_mix_post", "norm_mlp_pre", "norm_mlp_post")], 2).reshape(D, 128, 4 * NC_)
    consts = shape_constants()
    aux = np.zeros((D, HEADS, 128, AUXW), np.float32)
    aux[:, :H_C, :, AUX_GAIN] = a["norm_gdn"][:, None, :]
    aux[:, H_C:H_C + H_B, :, AUX_GAIN] = a["norm_ret"].reshape(D, H_B, 128)
    aux[:, H_C + H_B:, :, AUX_GAIN] = a["norm_mlstm"].reshape(D, H_A, 128)
    aux[:, :H_C, :, AUX_TAP:AUX_TAP + 12] = a["gdn_conv_w"].reshape(D, CONVW, 3, H_C, 128).transpose(0, 3, 4, 2, 1).reshape(D, H_C, 128, 12)
    aux[:, H_C:H_C + H_B, :, AUX_TAP:AUX_TAP + 3] = consts.pop("k_kdec").transpose(1, 0, 2)
    aux[:, H_C:H_C + H_B, :, AUX_STATE:] = consts.pop("k_dmat").transpose(1, 0, 2)
    aux[:, :H_C, :, AUX_STATE:AUX_STATE + CONVS] = a["state_gdn_conv"].reshape(D, NB, CONVW - 1, 3, H_C, 128).transpose(0, 4, 5, 3, 1, 2).reshape(D, H_C, 128, -1)
    aux[:, H_C + H_B:, :, AUX_STATE:AUX_STATE + NB] = a["state_mlstm_n"].transpose(0, 2, 3, 1)
    sin = np.concatenate([a[k].transpose(0, 2, 3, 1, 4) for k in ("state_gdn_S", "state_ret_S", "state_mlstm_C")], 1)
    x = np.concatenate([a["x_prompt"].reshape(SEQ, NC_, 128), a["x_sample"].reshape(NS, NC_, 128)]).transpose(2, 1, 0)

    feed = {
        "w": w, "x": x, "gw": gw, "gp": gp, "ng": ng, "mi": a["state_mlstm_m"].transpose(0, 2, 1),
        "aux": aux.reshape(D * HEADS, 128, AUXW), "sin": sin.reshape(D * HEADS, 128, NB * HD), **consts,
    }
    outs = {
        "y": (128, NC_, T), "sout": (D * HEADS, 128, (1 + NB) * HD), "nout": (D * H_A, 128, 1 + NB),
        "mo": (D, H_A, 1 + NB), "cnew": (D * H_C, 128, 3 * (1 + NB) * (CONVW - 1)),
    }
    nc = _bacc.Bacc("TRN2", target_bir_lowering=False, num_devices=1)
    arrays, d = {}, {}
    for k, v in feed.items():
        v = np.ascontiguousarray(v)
        arrays[f"in_{k}"] = v
        d[k] = nc.dram_tensor(f"in_{k}", v.shape, F32, kind="ExternalInput").ap()
    for k, shape in outs.items():
        d[k] = nc.dram_tensor(f"out_{k}", shape, F32, kind="ExternalOutput").ap()
    d["bc"] = nc.dram_tensor("gate_rows", (D * HEADS, BCW), F32, kind="Internal").ap()
    build(nc, d)
    r = _run(nc, [arrays], core_ids=[0]).results[0]

    y = r["out_y"].transpose(2, 1, 0).reshape(T, D_MODEL)
    so = r["out_sout"].reshape(D, HEADS, 128, 1 + NB, HD).transpose(0, 3, 1, 2, 4)
    no = r["out_nout"].reshape(D, H_A, 128, 1 + NB).transpose(0, 3, 1, 2)
    mo = r["out_mo"].transpose(0, 2, 1)
    co = r["out_cnew"].reshape(D, H_C, 128, 3, 1 + NB, CONVW - 1).transpose(0, 4, 5, 3, 1, 2)
    co = co.reshape(D, 1 + NB, CONVW - 1, 3 * H_C * HD)
    res = [y[:SEQ].reshape(1, SEQ, D_MODEL), y[SEQ:].reshape(NB, DS, D_MODEL)]
    for b in (slice(0, 1), slice(1, None)):
        res += [so[:, b, H_C + H_B:], no[:, b], mo[:, b], so[:, b, H_C:H_C + H_B], so[:, b, :H_C], co[:, b]]
    return tuple(np.ascontiguousarray(v) for v in res)
```

```python
from contextlib import ExitStack

import numpy as np

import concourse.bass as bass
from concourse import mybir

F32 = mybir.dt.float32
F32R = mybir.dt.float32r
ACT = mybir.ActivationFunctionType
ALU = mybir.AluOpType

DEPTH = 2
D_MODEL = 2048
D_FF = 4 * D_MODEL
HD = 128
SEQ = 256
NB = 8
DS = 4
NS = NB * DS
T = SEQ + NS
TILES = ((0, 128, 128), (128, 256, 128), (256, 288, 32))
NC_ = D_MODEL // HD
H_C, H_B, H_A = 8, 4, 4
HEADS = H_C + H_B + H_A
SCALE = HD ** -0.5
EPS = 1e-6
SOFTCAP = 15.0
PAST_LEN = 2048
CONVW = 4
QUADS = HEADS + NC_ // 4 + 2 * D_FF // HD // 4
MLP_Q = D_FF // D_MODEL
SLOTS = 32
LEVELS = 7
BIG = -1e30
CAP = 2.0 ** 62
CB_P = SEQ + CONVW - 1
CB_N = CB_P + NB * (DS + CONVW - 1)
CO = CB_N - (CONVW - 1)
EXT_P = SEQ + 1
EXT = EXT_P + NB * (DS + 1)
AUX_GAIN, AUX_TAP, AUX_STATE = 0, 1, 16
AUXW = AUX_STATE + T
CONVS = 3 * NB * (CONVW - 1)
BCW = 2 * T + NS


INVERSE_SLOT = 5
CONV_SLOTS = (8, 16, 24)
EXP_AFTER, LOG_AFTER, TAPS_A_SLOT = (4, 4, 3), (5, 5, 4), (1, 1, 2)


LINEAR_SLOTS = {0: 1, 1: 2, 2: 4, 3: 6, 4: 8, 5: 9, 8: 12, 10: 15}
LAST_SLOTS = {0: 0, 1: 1, 2: 2, 3: 3, 4: 4, 5: 5, 8: 6, 10: 6}


def shape_constants():
    f = np.float32
    half = HD // 2
    inv = np.power(f(10000.0), -np.arange(half, dtype=f) / f(half)).astype(f)
    pos = np.concatenate([np.arange(SEQ), np.tile(PAST_LEN + np.arange(DS), NB)]).astype(f)
    ang = (pos[None, :] * inv[:, None]).astype(f)
    cos, sin = np.cos(ang).astype(f), np.sin(ang).astype(f)
    ident = np.eye(HD, dtype=f)
    rot = np.zeros((HD, HD), f)
    rot[np.arange(half) + half, np.arange(half)] = -1.0
    rot[np.arange(half), np.arange(half) + half] = 1.0
    i = np.arange(HD)
    seq = np.arange(NS) // DS
    causal = (i[None, :] >= i[:, None]).astype(f)
    causal_s = np.zeros((HD, NS), f)
    causal_s[:NS] = (seq[None, :] == seq[:, None]) * (np.arange(NS)[None, :] >= np.arange(NS)[:, None])
    own = np.zeros((HD, NB), f)
    own[np.arange(NS), seq] = 1.0
    levels = np.stack([((i[:, None] // (2 * b) == i[None, :] // (2 * b)) & (i[:, None] % (2 * b) < b)
                        & (i[None, :] % (2 * b) >= b)).astype(f) for b in (2 ** n for n in range(LEVELS))], 1)
    lg = np.log1p(-np.exp2(-5.0 - np.arange(H_B, dtype=np.float64)))
    t = np.arange(SEQ)
    dmat = np.zeros((HD, H_B, T), f)
    kdec = np.zeros((HD, H_B, 3), f)
    rdec = np.zeros((HD, H_B, NS), f)
    for h in range(H_B):
        dist = t[None, :] - i[:, None]
        dmat[:, h, :SEQ] = np.where(dist >= 0, np.exp(np.maximum(dist, 0) * lg[h]), 0.0)
        ds = np.arange(NS)[None, :] - np.arange(NS)[:, None]
        dmat[:NS, h, SEQ:] = causal_s[:NS] * np.exp(np.maximum(ds, 0) * lg[h])
        kdec[:, h, 0] = np.exp((SEQ - 1 - i) * lg[h]) * SCALE
        kdec[:, h, 1] = np.exp((HD - 1 - i) * lg[h]) * SCALE
        kdec[:NS, h, 2] = np.exp((DS - 1 - np.arange(NS) % DS) * lg[h]) * SCALE
        rdec[:, h] = np.exp((np.arange(NS) % DS + 1) * lg[h])
    resets = np.ones((HD, T), f)
    resets[:, 0] = 0.0
    resets[:, SEQ::DS] = 0.0
    resets[64:, HD] = 0.0
    rows = np.zeros((H_B, BCW), f)
    rows[:, 2 * T:] = rdec[0]
    return {
        "k_rows": rows, "k_kdec": kdec,
        "c_ident": ident, "c_rot": rot, "c_center": ident - f(1.0 / HD), "c_causal": causal,
        "c_never": (1.0 - causal) * f(BIG), "c_causal_s": causal_s, "c_never_s": (1.0 - causal_s) * f(BIG),
        "c_own": own, "c_levels": levels, "c_cos": np.concatenate([cos, cos]), "c_sin": np.concatenate([sin, sin]),
        "k_dmat": dmat, "k_resets": resets,
    }


def build(nc, d):
    with ExitStack() as ctx:
        def sb(name, shape, dt=F32):
            return ctx.enter_context(nc.sbuf_tensor(name, shape, dt))

        sems = {}

        def sem(name):
            if name not in sems:
                sems[name] = ctx.enter_context(nc.semaphore(name))
            return sems[name]

        X = sb("X", [128, NC_, T])
        Y = sb("Y", [128, NC_, T])
        HH, HL = sb("HH", [128, NC_, T], F32R), sb("HL", [128, NC_, T], F32R)
        UH, UL = sb("UH", [128, NC_, T], F32R), sb("UL", [128, NC_, T], F32R)
        RAW = [sb(f"RAW{i}", [128, NC_ // 4, HD]) for i in range(4)]
        WH = [sb(f"WH{i}", [128, NC_, HD], F32R) for i in range(2)]
        WL = [sb(f"WL{i}", [128, NC_, HD], F32R) for i in range(2)]
        con = {n: sb(n, list(d[n].shape)) for n in d if n.startswith("c_")}
        IDENT, OWN = con["c_ident"], con["c_own"]
        ONES = sb("ONES", [128, HD])
        S, RS = sb("S", [128, T]), sb("RS", [128, T])
        EPSC = sb("EPSC", [128, 1])
        ONEC = sb("ONEC", [128, 1])
        NG = sb("NG", [128, 3, NC_])
        NG0 = sb("NG0", [128, NC_])
        GP = sb("GP", [128, 2])
        MI = sb("MI", [H_A, NB])
        Z = [sb(f"Z{i}", [128, 4, T]) for i in range(2)]
        AUX = [sb(f"AUX{i}", [128, AUXW]) for i in range(2)]
        BC = [sb(f"BC{i}", [128, BCW]) for i in range(2)]
        SIN = sb("SIN", [128, NB, HD])
        SOUT = sb("SOUT", [128, HD])
        NOUT = sb("NOUT", [128, 1 + NB])
        CNEW = sb("CNEW", [128, 3, (1 + NB) * (CONVW - 1)])
        MOUT = sb("MOUT", [H_A, 1 + NB])
        COLA, COLB = sb("COLA", [128, 3, 128]), sb("COLB", [128, 3, 128])
        CUR = sb("CUR", [128, 3, 3])
        ybase = [0]

        def scratch(shape):
            n = int(np.prod(shape[1:]))
            a = Y[0:shape[0]].rearrange("p c t -> p (c t)")[:, ybase[0]:ybase[0] + n]
            ybase[0] += n
            if len(shape) == 3:
                a = a.rearrange("p (a b) -> p a b", b=shape[2])
            return a

        CDEC = scratch([128, NB, HD])
        VEXP = scratch([128, NB, HD])
        TR = scratch([128, 4, HD])
        V_ = scratch([128, 3, HD])
        KW = scratch([128, 3, HD])
        U_ = scratch([128, 3, HD])
        QK2 = scratch([128, 2, T])
        DX = scratch([128, T])
        assert ybase[0] <= NC_ * T
        CB = sb("CB", [128, 3, CB_N])
        CB0 = CB[:, :, 0:CONVW - 1]
        AE = sb("AE", [128, 6, CO])
        ACC, EE = AE[:, 0:3], AE[:, 3:6]
        QKG = sb("QKG", [128, 2, T])
        AM = sb("AM", [128, T])
        SC = sb("SC", [128, 416])
        PM = sb("PM", [128, T])
        S1 = sb("S1", [128, HD])
        RHS = sb("RHS", [128, 2, HD])
        TS = sb("TS", [NS, 2, NS])
        SMALL = sb("SMALL", [128, 2, NS])
        SQH, LG, GATE = [sb(n, [128, T]) for n in ("SQH", "LG", "GATE")]
        HHD, YY = AM, PM
        LW = EE.rearrange("p a b -> p (a b)")[:, 0:416]
        SQ = AE[:].rearrange("p a b -> p (a b)")[:, 0:4 * T].rearrange("p (a b) -> p a b", b=T)
        GWf = Y[:].rearrange("p c t -> p (c t)")[:, 0:NC_ * HD].rearrange("p (c m) -> p c m", m=HD)
        RESETS = Y[:].rearrange("p c t -> p (c t)")[:, 2560:2560 + T]
        yf = Y[:].rearrange("p c t -> p (c t)")
        ZG, GE, GT, GU = SC[:, 0:T], PM[:], DX, QKG[:, 0]
        ROWA, ROWB = Z[1][:, 3], yf[:, 1024:1024 + T]
        AR, EM, IR = [Z[1][0:H_A, j] for j in range(3)]
        EXTF, EXTI, EXTM = [yf[0:H_A, j:j + EXT] for j in (2048, 2848, 2848 + EXT)]
        F0, MC = QKG[0:H_A, 1], AM[0:H_A, :]
        UPE = [ACC[:, 0, 0:T], ACC[:, 1, 0:T]]
        UPT = [EE[:, 0, 0:T], EE[:, 1, 0:T]]

        PU = [ctx.enter_context(nc.psum_tensor(f"PU{i}", [128, 512], F32)) for i in range(2)]
        PAB = ctx.enter_context(nc.psum_tensor("PAB", [128, 2, 512], F32))
        PCD = ctx.enter_context(nc.psum_tensor("PCD", [128, 2, 512], F32))
        PE_ = ctx.enter_context(nc.psum_tensor("PE_", [128, 512], F32))
        PF = ctx.enter_context(nc.psum_tensor("PF", [128, 512], F32))
        PA, PB, PC, PD = PAB[:, 0], PAB[:, 1], PCD[:, 0], PCD[:, 1]
        print("sbuf left", nc.sbuf_bytes_remaining() if callable(nc.sbuf_bytes_remaining) else nc.sbuf_bytes_remaining)

        def sview(a):
            return a[:, SEQ:T].rearrange("p (b t) -> p b t", t=DS)

        def walk(eng, start, quad, after_out, after_mlp):
            with eng.Fori(0, DEPTH) as l:
                q0, n0, p0 = l * QUADS, l * HEADS, l * (HEADS // 2)
                if start:
                    start(l)
                quad(q0, "first", l, None, (n0, l * H_C, 0, 0, p0))

                def gdn_pair(i, last):
                    for par in range(2):
                        h = 2 * i + par
                        after = None if last and par else (n0 + h + 1, l * H_C + h + 1, h + 1, 1 - par, p0 + i + par)
                        quad(q0 + 1 + h, "gdn", l, (n0 + h, l * H_C + h, h, par, p0 + i), after)

                with eng.Fori(0, H_C // 2 - 1) as i:
                    gdn_pair(i, False)
                gdn_pair(H_C // 2 - 1, True)
                with eng.Fori(0, H_B // 2) as i:
                    for par in range(2):
                        h = 2 * i + par
                        quad(q0 + 1 + H_C + h, "ret", l, (n0 + H_C + h, l * H_B + h, h, par, p0 + H_C // 2 + i))
                for h in range(H_A - 1):
                    quad(q0 + 1 + H_C + H_B + h, "mls", l, (n0 + H_C + H_B + h, l * H_A + h, h, h % 2, p0 + (H_C + H_B + h) // 2))
                h = H_A - 1
                last_head = (n0 + H_C + H_B + h, l * H_A + h, h, h % 2, p0 + (H_C + H_B + h) // 2)
                quad(q0 + HEADS, "out", l, (0, 0), last_head=last_head)
                with eng.Fori(1, NC_ // 4) as j:
                    quad(q0 + HEADS + j, "out", l, (0, j))
                after_out(l)
                base = q0 + HEADS + NC_ // 4
                quad(base, "up_first", l, (0, 0))
                with eng.Fori(1, NC_ // 4) as j:
                    quad(base + j, "up", l, (0, j))
                with eng.Fori(0, NC_ // 4) as j:
                    quad(base + 4 + j, "down0", l, (0, j))
                with eng.Fori(0, MLP_Q - 2) as q:
                    with eng.Fori(0, NC_ // 4) as j:
                        quad(base + 8 + 8 * q + j, "up", l, (q + 1, j))
                    with eng.Fori(0, NC_ // 4) as j:
                        quad(base + 12 + 8 * q + j, "down", l, (q + 1, j))
                q = MLP_Q - 2
                with eng.Fori(0, NC_ // 4) as j:
                    quad(base + 8 + 8 * q + j, "up", l, (q + 1, j))
                quad(base + 12 + 8 * q, "down_last", l, (q + 1, 0))
                with eng.Fori(1, NC_ // 4) as j:
                    quad(base + 12 + 8 * q + j, "down_last", l, (q + 1, j))
                after_mlp(l)

        def ul_before(l, kind, q):
            return l * (NC_ * (1 + MLP_Q)) + (0 if kind == "out" else NC_ * (q + 1))

        gate_steps = {
            "pe": ["proj", "turned"],
            "act": ["rate", "tanh_exp", "idle_rows", "beta_exp", "sp_exp", "log", "gamma", "kd_exp", "em", "wl_exp", "inter"],
            "dve": ["weights", "z", "biased", "rec_sum", "rec_sum", "rec", "capped", "beta", "y", "abs", "u", "rest",
                    "log1p", "softplus", "decay", *["ext"] * 4, "ext_f", *["ext"] * 2, *["scan"] * 2, "i", "f", *["m"] * 2,
                    "sums", *["mout"] * 2, "rows", *["kd_log"] * 3, "a", "b", *["wl_log"] * 2, "inter_log", "wl",
                    *["cols"] * 4],
        }

        def gate(name, l):
            engine = next(e for e, steps in gate_steps.items() if name in steps)
            steps = gate_steps[engine]
            return sem(f"gate_steps_{engine}"), l * len(steps) + len(steps) - steps[::-1].index(name)

        def aux_count(kind, x):
            n, nk, hk, par, pair = x
            return 16 * (pair + 1)

        def up_units(l, x, s):
            q, j = x
            return (l * MLP_Q + q) * NC_ + 4 * j + s

        block = ctx.enter_context(nc.Block())

        @block.sync
        def _(sp):
            def load(c, unit):
                k = slice(4 * c, 4 * c + 4)
                src = d["w"][unit, :, k] if isinstance(unit, int) else d["w"][bass.ds(unit, 1), :, k].rearrange("a p k m -> p (a k) m")
                sp.dma_start(RAW[c][:], src).then_inc(sem(f"raw_in{c}"), 16)

            for c in range(4):
                k = slice(4 * c, 4 * c + 4)
                sp.dma_start(X[:, k], d["x"][:, k]).then_inc(sem(f"x_in{c}"), 16)
                load(c, 0)
            for n in con:
                sp.dma_start(con[n][:], d[n]).then_inc(sem("constants_in"), 16)
            with sp.Fori(0, DEPTH * QUADS) as Q:
                for s in range(4):
                    for c in range(4):
                        sp.wait_ge(sem("lo_ready"), 16 * Q + 4 * s + c + 1)
                        load(c, 4 * Q + s + 1)
            sp.wait_ge(sem("lo_ready"), 16 * DEPTH * QUADS + 1)
            load(0, 4 * DEPTH * QUADS + 1)
            for g in range(4):
                sp.wait_ge(sem("x_updated"), 16 * DEPTH + 2 * g + 2)
                k = slice(4 * g, 4 * g + 4)
                sp.dma_start(d["y"][:, k], X[:, k]).then_inc(sem("y_stored"), 16)
            sp.wait_ge(sem("y_stored"), 16 * 4)

        @block.gpsimd
        def _(pool):
            def held(name, value):
                pool.wait_ge(sem(name) if isinstance(name, str) else name, value)
                pool.sem_inc(sem("pool_passes"), 1)

            def one(name, n):
                return d[name][bass.ds(n, 1)].rearrange("a p w -> p (a w)")

            def load_parameters(n, par):
                pool.dma_start(AUX[par][:], one("aux", n)).then_inc(sem(f"aux_in{par}"), 16)

            def load_rows(n, par):
                pool.dma_start(BC[par][:], d["bc"][bass.ds(n, 1)].rearrange("a t -> (a t)")
                               .partition_broadcast(128)).then_inc(sem(f"bc_in{par}"), 16)

            def load_state(n):
                pool.dma_start(SIN[:].rearrange("p b e -> p (b e)"), one("sin", n)).then_inc(sem("state_in"), 16)

            def head(l, n, pair, par, next_head):
                if next_head:
                    held("head_done", n + 1)
                    load_parameters(n + 1, 1 - par)
                    load_rows(n + 1, 1 - par)
                pool.wait_ge(sem(f"bc_in{par}"), 16 * (pair + 1))
                pool.wait_ge(sem("state_in"), 16 * (n + 1))
                pool.wait_ge(sem("state_ready"), n + 1)
                dec = BC[par][:, 2 * T + DS - 1:BCW:DS].unsqueeze(2).to_broadcast([128, NB, HD])
                pool.tensor_tensor(CDEC, SIN[:], dec, ALU.mult).then_inc(sem("state_decayed"), 1)
                pool.wait_ge(sem("sample_values"), n + 1)
                pool.tensor_tensor(VEXP[0:NS], U_[0:NS, 2].unsqueeze(1).to_broadcast([NS, NB, HD]),
                                   OWN[0:NS].unsqueeze(2).to_broadcast([NS, NB, HD]), ALU.mult).then_inc(sem("values_spread"), 1)
                if next_head:
                    held("state_decayed", n + 1)
                    held("state_read", n + 1)
                    load_state(n + 1)
                held("state_ready", n + 2)
                pool.dma_start(one("sout", n)[:, HD:], CDEC.rearrange("p b e -> p (b e)")).then_inc(sem("state_out"), 16)
                held("state_out", 16 * (n + 1))

            pool.dma_start(NG0[:], d["ng0"][0]).then_inc(sem("first_gain_in"), 16)
            held("constants_in", 16 * len(con))
            for name in ("prompt_out", "norm_out", "cnew_out"):
                pool.sem_inc(sem(name), 16)
            for l in range(DEPTH):
                pool.dma_start(d["bc"][l * HEADS + H_C:l * HEADS + H_C + H_B], d["k_rows"]).then_inc(sem("ret_rows_out"), 16)
            held("ret_rows_out", 16 * DEPTH)
            with pool.Fori(0, DEPTH) as l:
                n0, p0 = l * HEADS, l * (HEADS // 2)
                held("layer_free", l + 1)
                pool.dma_start(GWf, d["gw"][bass.ds(l, 1)].rearrange("a p c m -> p (a c) m")).then_inc(sem("gate_in"), 16)
                pool.dma_start(NG[:].rearrange("p k c -> p (k c)"), one("ng", l)).then_inc(sem("gains_in"), 16)
                pool.dma_start(GP[:], one("gp", l)).then_inc(sem("gate_in"), 16)
                pool.dma_start(MI[:], one("mi", l)).then_inc(sem("gate_in"), 16)
                pool.dma_start(RESETS, d["k_resets"]).then_inc(sem("gate_in"), 16)
                load_parameters(n0, 0)
                held(*gate("em", l))
                held(*gate("inter", l))
                held(*gate("a", l))
                held(*gate("rows", l))
                held(*gate("gamma", l))
                held(*gate("mout", l))
                a0 = n0 + H_C + H_B
                rows_a, rows_c = d["bc"][bass.ds(a0, H_A)], d["bc"][bass.ds(n0, H_C)]
                pool.dma_start(rows_a[:, 0:T], AR[:]).then_inc(sem("rows_out"), 16)
                pool.dma_start(rows_a[:, T:2 * T], EM[:]).then_inc(sem("rows_out"), 16)
                pool.dma_start(rows_a[:, 2 * T:], IR[:, SEQ:T]).then_inc(sem("rows_out"), 16)
                pool.dma_start(rows_c[:, 0:T], ROWA[64:64 + H_C]).then_inc(sem("rows_out"), 16)
                pool.dma_start(rows_c[:, T:2 * T], GT[64:64 + H_C]).then_inc(sem("rows_out"), 16)
                pool.dma_start(rows_c[:, 2 * T:], GT[64:64 + H_C, SEQ:T]).then_inc(sem("rows_out"), 16)
                pool.dma_start(one("mo", l), MOUT[:]).then_inc(sem("rows_out"), 16)
                held("rows_out", 16 * 7 * (l + 1))
                load_rows(n0, 0)
                load_state(n0)
                pool.dma_start(NG0[:], one("ng0", l + 1)).then_inc(sem("first_gain_in"), 16)
                with pool.Fori(0, (H_C + H_B) // 2) as i:
                    for par in range(2):
                        head(l, n0 + 2 * i + par, p0 + i, par, True)
                for h in range(H_A):
                    head(l, a0 + h, p0 + (H_C + H_B) // 2 + h // 2, h % 2, h < H_A - 1)
            pool.wait_ge(sem("first_gain_in"), 16 * (DEPTH + 1))
            pool.wait_ge(sem("state_out"), 16 * DEPTH * HEADS)
            pool.wait_ge(sem("rows_out"), 16 * 7 * DEPTH)

        @block.tensor
        def _(pe):
            def mm(out, lhsT, rhs, start=True, stop=True):
                return nc.tensor.matmul(out, lhsT, rhs, start=start, stop=stop, skip_group_check=True)

            def unit_part(Q, t, kind, l, x):
                s, kk = divmod(t, 8)
                hi, lo = (UH, UL) if kind in ("out", "down", "down0", "down_last") else (HH, HL)
                if kk == 0:
                    pe.wait_ge(sem("psum_read"), 4 * Q + s + 1)
                if kk % 2 == 0:
                    pe.wait_ge(sem("lo_ready"), 16 * Q + 4 * s + kk // 2 + 1)
                for k in (2 * kk, 2 * kk + 1):
                    if s == 0:
                        if kind == "first":
                            pe.wait_ge(sem("hl_ready"), 2 * l * NC_ + k + 1)
                        elif kind in ("out", "down", "down0", "down_last"):
                            pe.wait_ge(sem("ul_ready"), ul_before(l, kind, x[0]) + k + 1)
                        elif kind == "up_first":
                            pe.wait_ge(sem("hl_ready"), (2 * l + 1) * NC_ + k + 1)
                    mm(PU[s % 2][:, 0:T], WH[s % 2][:, k], hi[:, k], k == 0, False)
                    mm(PU[s % 2][:, 0:T], WH[s % 2][:, k], lo[:, k], False, False)
                    last = mm(PU[s % 2][:, 0:T], WL[s % 2][:, k], hi[:, k], False, k == NC_ - 1)
                if kk == 7:
                    last.then_inc(sem("unit_done"), 1)

            def norm_sum(e, c, slot, first=False, last=False):
                pe.wait_ge(sem("squares"), NC_ * e + c + 1)
                mm(PC[:, 0:T], ONES[:], SQ[:, slot], first, last).then_inc(sem("squares_summed"), 1)

            def norm_part(t, kind, l, x):
                if kind in ("first", "up_first") and t < 8:
                    for c in (2 * t, 2 * t + 1):
                        norm_sum(4 * l + (2 if kind == "up_first" else 0), c, c % 4, c == 0, c == NC_ - 1)
                if kind in ("out", "down_last") and t % 8 == 3:
                    first = isinstance(x[1], int)
                    units = {0: (), 1: (), 2: (0, 1), 3: (2,)}[t // 8] if first else (t // 8 - 1,)
                    for s in units:
                        norm_sum(4 * l + (1 if kind == "out" else 3), 4 * x[1] + s, s % 4, first and s == 0)

            def gates(t, l):
                if t == 8:
                    pe.wait_ge(sem("constants_in"), 16 * len(con))
                    pe.wait_ge(*gate("weights", l))
                if 8 <= t < 16:
                    for k in (2 * t - 16, 2 * t - 15):
                        i = mm(PD[:, 0:T], GWf[:, k], X[:, k], k == 0, k == NC_ - 1)
                    if t == 15:
                        i.then_inc(gate("proj", 0)[0], 1)
                if t == 31:
                    pe.wait_ge(sem("gdn_l2_log"), 2 * (l * H_C + 1))
                    pe.wait_ge(*gate("wl", l))
                    pe.wait_ge(*gate("beta", l))
                    pe.wait_ge(*gate("kd_exp", l))
                    pe.wait_ge(*gate("rows", l))
                    pe.wait_ge(*gate("b", l))
                    for dst, src in ((PE_, ROWA), (PF, ROWB)):
                        for j, (a, b, m) in enumerate(TILES):
                            i = mm(dst[0:m, j * HD:(j + 1) * HD], src[:, a:b], IDENT[:])
                    i.then_inc(gate("turned", 0)[0], 1)
                    pe.wait_ge(*gate("cols", l))
                    pe.sem_inc(sem("pe_passes"), 1)

            def linear_head(step, kind, x):
                n, nk, hk, par, pair = x
                mls = kind == "mls"
                z = Z[par]
                q, k = (z[:, 0], z[:, 1]) if mls else (QK2[:, 0], QK2[:, 1])
                v = z[:, 2]
                if step == 0:
                    pe.wait_ge(sem("head_done"), n + 1)
                if step == 0 and not mls:
                    pe.wait_ge(sem("z_ready"), 4 * n + 4)
                    mm(PC[:, 0:T], con["c_rot"][:], z[:, 0])
                    mm(PD[:, 0:T], con["c_rot"][:], z[:, 1]).then_inc(sem("ret_rotated"), 1)
                if step == 2:
                    if mls:
                        pe.wait_ge(sem("z_ready"), 4 * n + 4)
                    else:
                        pe.wait_ge(sem("ret_qk"), 3 * (nk + 1))
                    pe.wait_ge(sem("state_ready"), n + 1)
                    for dst, src in ((PA, k), (PB, v)):
                        for j, (a, b, m) in enumerate(TILES):
                            last = mm(dst[0:m, j * HD:(j + 1) * HD], src[:, a:b], IDENT[:])
                    last.then_inc(sem("kv_turned"), 1)
                    mm(PE_[:, 0:SEQ], k[:, 0:HD], q[:, 0:SEQ])
                    mm(PE_[:, SEQ:SEQ + HD], k[:, HD:SEQ], q[:, HD:SEQ])
                    mm(PE_[0:NS, 384:416], k[:, SEQ:T], q[:, SEQ:T]).then_inc(sem("scores"), 1)
                if step == 3:
                    pe.wait_ge(sem(f"{kind}_probs"), (2 if mls else 3) * (nk + 1))
                    pe.wait_ge(sem(f"{kind}_kept"), 5 * (nk + 1))
                    pe.wait_ge(sem(f"{kind}_qs"), nk + 1)
                    pe.wait_ge(sem("state_in"), 16 * (n + 1))
                    mm(PF[:, 0:SEQ], U_[:, 0], SC[:, 0:SEQ], True, False)
                    mm(PF[:, HD:SEQ], U_[:, 1], SC[:, SEQ:SEQ + HD], False, False)
                    for b in range(NB):
                        c = slice(SEQ + DS * b, SEQ + DS * b + DS)
                        i = mm(PF[:, c], SIN[:, b], SMALL[:, 0, DS * b:DS * b + DS], False, False)
                    i.then_inc(sem("state_read"), 1)
                    i = mm(PF[:, SEQ:T], U_[0:NS, 2], SC[0:NS, 384:416], False, True)
                    if mls:
                        pe.wait_ge(sem("mls_qn"), nk + 1)
                        mm(PC[:, 0:SEQ], ONES[:], SC[:, 0:SEQ], True, False)
                        mm(PC[:, HD:SEQ], ONES[:], SC[:, SEQ:SEQ + HD], False, False)
                        mm(PC[:, SEQ:T], ONES[:], SMALL[:, 1], False, False)
                        i = mm(PC[:, SEQ:T], ONES[0:NS], SC[0:NS, 384:416], False, True)
                    i.then_inc(sem(f"{kind}_out"), 1)
                    mm(PD[:, 0:HD], KW[:, 0], U_[:, 0], True, False)
                    i = mm(PD[:, 0:HD], KW[:, 1], U_[:, 1], False, True)
                    if mls:
                        mm(PD[:, HD:HD + 1], KW[:, 0], ONES[:, 0:1], False, False)
                        mm(PD[:, HD:HD + 1], KW[:, 1], ONES[:, 0:1], False, True)
                        i = mm(PD[:, HD + 1:HD + 1 + NB], KW[0:NS, 2], OWN[0:NS], False, True)
                    i.then_inc(sem("prompt_state"), 1)
                if step == 4 and not mls:
                    pe.wait_ge(sem("ret_kept_out"), nk + 1)
                    mm(PC[:, 0:T], con["c_center"][:], YY[:]).then_inc(sem("ret_centered"), 1)
                if step == 8:
                    if mls:
                        pe.wait_ge(sem("mls_nout"), 3 * (nk + 1))
                    head_sums(n)
                if step == 10:
                    sample_state(n)

            def head_sums(n):
                pe.wait_ge(sem("head_squares"), n + 1)
                pe.wait_ge(sem("state_kept"), n + 1)
                mm(PD[:, 0:T], ONES[:], SQH[:]).then_inc(sem("head_sums"), 1)

            def sample_state(n):
                pe.wait_ge(sem("values_spread"), n + 1)
                mm(PA, KW[0:NS, 2], VEXP[0:NS, 0:4].rearrange("p b e -> p (b e)"))
                mm(PB, KW[0:NS, 2], VEXP[0:NS, 4:8].rearrange("p b e -> p (b e)")).then_inc(sem("sample_state"), 1)

            def gdn_front(t, x):
                n, nk, hk, par, pair = x
                for c, slot in ((0, 20), (1, 24)):
                    if t == slot:
                        pe.wait_ge(sem("gdn_squares"), 2 * nk + c + 1)
                        if c:
                            pe.wait_ge(sem("gdn_l2_log"), 2 * nk + 1)
                        mm(PE_[:, 0:T], ONES[:], EE[:, c, 0:T]).then_inc(sem("gdn_sums"), 1)

            def gdn_head(t, x):
                n, nk, hk, par, pair = x
                v = Z[par][:, 2]
                if t == 2:
                    pe.wait_ge(sem("gdn_qk"), 2 * (nk + 1))
                    pe.wait_ge(sem("gdn_qkv"), 6 * (nk + 1))
                    pe.wait_ge(sem("state_ready"), n + 1)
                    k = QK2[:, 1]
                    for dst, src in ((PA, k), (PB, v)):
                        for j, (a, b, m) in enumerate(TILES):
                            last = mm(dst[0:m, j * HD:(j + 1) * HD], src[:, a:b], IDENT[:])
                    last.then_inc(sem("kv_turned"), 1)
                if t == 3:
                    q, k = QK2[:, 0], QK2[:, 1]
                    for a, b, m in TILES:
                        i = mm(PC[0:m, a:b], k[:, a:b], k[:, a:b])
                    i.then_inc(sem("gdn_kk"), 1)
                    for a, b, m in TILES:
                        i = mm(PF[0:m, a:b], k[:, a:b], q[:, a:b])
                    i.then_inc(sem("scores"), 1)
                if INVERSE_SLOT <= t < INVERSE_SLOT + 2 * LEVELS:
                    lev, second = divmod(t - INVERSE_SLOT, 2)
                    R = [IDENT[:], IDENT[:]] if lev == 0 else [TR[:, 1], TR[:, 3]]
                    TT = [IDENT[:], IDENT[:]] if lev == 0 else [TR[:, 0], TR[:, 2]]
                    Rs = IDENT[0:NS, 0:NS] if lev == 0 else TS[:, 1]
                    Ts = IDENT[0:NS, 0:NS] if lev == 0 else TS[:, 0]
                    if not second:
                        if lev == 0:
                            pe.wait_ge(sem("head_done"), n + 1)
                            pe.wait_ge(sem("gdn_A"), 3 * (nk + 1))
                        else:
                            pe.wait_ge(sem("gdn_inverse"), LEVELS * nk + lev)
                        for j in range(2):
                            i = mm(PD[:, j * HD:(j + 1) * HD], AM[:, j * HD:(j + 1) * HD], R[j])
                        if lev < 2:
                            i = mm(PD[0:NS, SEQ:T], AM[0:NS, SEQ:T], Rs)
                        i.then_inc(sem("gdn_P"), 1)
                    else:
                        pe.wait_ge(sem("gdn_Pm"), LEVELS * nk + lev + 1)
                        for j in range(2):
                            p = PM[:, j * HD:(j + 1) * HD]
                            if lev < LEVELS - 1:
                                mm(PE_[:, 2 * j * HD:(2 * j + 1) * HD], p, TT[j])
                            i = mm(PE_[:, (2 * j + 1) * HD:(2 * j + 2) * HD], TT[j], p)
                        if lev < 2:
                            mm(PC[0:NS, 0:NS], PM[0:NS, SEQ:T], Ts)
                            i = mm(PC[0:NS, NS:2 * NS], Ts, PM[0:NS, SEQ:T])
                        i.then_inc(sem("gdn_TR"), 1)
                if t == 19:
                    pe.wait_ge(sem("gdn_inverse"), LEVELS * (nk + 1))
                    pe.wait_ge(sem("gdn_kept"), 6 * (nk + 1))
                    mm(PA[:, 0:HD], TR[:, 1], V_[:, 0]).then_inc(sem("gdn_u0"), 1)
                    pe.wait_ge(sem("gdn_qkg"), 2 * (nk + 1))
                    pe.wait_ge(sem("state_in"), 16 * (n + 1))
                    for b in range(NB):
                        out = PF[:, SEQ + DS * b:SEQ + DS * b + 2 * NS].rearrange("p (a c) -> p a c", c=NS)[:, :, 0:DS]
                        i = mm(out, SIN[:, b], QKG[:, :, SEQ + DS * b:SEQ + DS * b + DS], b == 0, False)
                    i.then_inc(sem("state_read"), 1)
                if t == 20:
                    pe.wait_ge(sem("gdn_u0_kept"), nk + 1)
                    mm(PB[:, 0:HD], KW[:, 0], U_[:, 0]).then_inc(sem("gdn_s1"), 1)
                    pe.wait_ge(sem("gdn_ks_kept"), nk + 1)
                    mm(PC[0:NS, 0:HD], SMALL[:, 0], IDENT[:]).then_inc(sem("gdn_ks_turned"), 1)
                if t == 22:
                    pe.wait_ge(sem("gdn_s1_kept"), nk + 1)
                    pe.wait_ge(sem("gdn_rhs_s"), nk + 1)
                    mm(PB[:, HD:2 * HD], QKG[:, 1, HD:SEQ], S1[:]).then_inc(sem("gdn_ks"), 1)
                    mm(PC[0:NS, HD:2 * HD], TS[:, 1], RHS[0:NS, 1]).then_inc(sem("gdn_us"), 1)
                if t == 24:
                    pe.wait_ge(sem("gdn_rhs"), nk + 1)
                    mm(PA[:, HD:2 * HD], TR[:, 3], RHS[:, 0]).then_inc(sem("gdn_u1"), 1)
                if t == 26:
                    pe.wait_ge(sem("gdn_u1_kept"), nk + 1)
                    mm(PB[:, 2 * HD:3 * HD], KW[:, 1], U_[:, 1]).then_inc(sem("prompt_state"), 1)
                    pe.wait_ge(sem("gdn_probs"), 2 * (nk + 1))
                    mm(PF[:, 0:HD], U_[:, 0], SC[:, 0:HD], False, False)
                    mm(PF[:, HD:SEQ], S1[:], QKG[:, 0, HD:SEQ], False, False)
                    mm(PF[:, HD:SEQ], U_[:, 1], SC[:, HD:SEQ], False, False)
                    pe.wait_ge(sem("sample_values"), n + 1)
                    mm(PF[:, SEQ:T], U_[0:NS, 2], SC[0:NS, SEQ:T], False, True).then_inc(sem("gdn_out"), 1)
                if t == 29:
                    head_sums(n)
                if t == 28:
                    pe.wait_ge(sem("state_kept"), n + 1)
                    sample_state(n)

            def mixer(t, kind, l, x, last=False):
                if kind == "gdn":
                    gdn_head(t, x)
                elif kind in ("ret", "mls"):
                    for step, slot in (LAST_SLOTS if last else LINEAR_SLOTS).items():
                        if t == slot:
                            linear_head(step, kind, x)
                elif kind == "first":
                    gates(t, l)

            def quad(Q, kind, l, x, front=None, last_head=None):
                for t in range(SLOTS):
                    unit_part(Q, t, kind, l, x)
                    norm_part(t, kind, l, x)
                    mixer(t, kind, l, x)
                    if last_head:
                        mixer(t, "mls", l, last_head, last=True)
                    if front:
                        gdn_front(t, front)

            pe.sem_inc(sem("unit_done"), 2)
            pe.sem_inc(sem("psum_read"), 2)
            pe.wait_ge(sem("ones_set"), 1)
            walk(pe, None, quad,
                 lambda l: norm_sum(4 * l + 1, NC_ - 1, 3, last=True), lambda l: norm_sum(4 * l + 3, NC_ - 1, 3, last=True))

        @block.scalar
        def _(act):
            act.preload_act_table_set("natural_log_exp_and_others")

            def fn(out, in_, f=ACT.Copy, **kw):
                return nc.scalar.activation(out, in_, f, **kw)

            def hi_part(Q, p):
                s, c = divmod(p, 4)
                act.wait_ge(sem(f"raw_in{c}"), 16 * (4 * Q + s + 1))
                if c == 0:
                    act.wait_ge(sem("unit_done"), 4 * Q + s + 1)
                k = slice(4 * c, 4 * c + 4)
                fn(WH[s % 2][:, k], RAW[c][:]).then_inc(sem("hi_ready"), 1)

            def prenorm(l, e, gain):
                if e == 0:
                    act.wait_ge(sem("first_gain_in"), 16 * (l + 1))
                else:
                    act.wait_ge(sem("gains_in"), 16 * (l + 1))
                for i in range(NC_ + 3):
                    c = i
                    if c < NC_:
                        if e == 0 and c % 4 == 0:
                            act.wait_ge(sem(f"x_in{c // 4}"), 16)
                        if c % 2 == 0:
                            act.wait_ge(sem("x_updated"), 16 * l + 4 * e + c // 2 + 1)
                        fn(HH[:, c], X[:, c], scale=gain[:, c:c + 1]).then_inc(sem("hh_ready"), 1)
                    c = i - 3
                    if c >= 4:
                        act.wait_ge(sem("squares_summed"), NC_ * (4 * l + e) + c - 3)
                    if c >= 0:
                        fn(SQ[:, c % 4], X[:, c], ACT.Square).then_inc(sem("squares"), 1)
                norm_scale(4 * l + e, S, "s_ready")

            def output_squares(t, kind, l, x):
                s = t // 8
                c = 4 * x[1] + s
                e = 4 * l + (1 if kind == "out" else 3)
                if not isinstance(x[1], int):
                    act.wait_ge(sem("squares_summed"), NC_ * e + c - 3)
                if kind == "out":
                    act.wait_ge(sem("y_ready"), l * NC_ + c + 1)
                else:
                    act.wait_ge(sem("y_added"), (l * MLP_Q + x[0]) * NC_ + c + 1)
                act.sem_inc(sem("act_passes"), 1)
                fn(SQ[:, s:s + 1].rearrange("p a t -> p (a t)"), Y[:, bass.ds(c, 1)].rearrange("p a t -> p (a t)"), ACT.Square)\
                    .then_inc(sem("squares"), 1)

            def norm_scale(e, dst, name):
                act.wait_ge(sem("squares_summed"), NC_ * (e + 1))
                fn(dst[:], PC[:, 0:T], ACT.Ln, scale=1.0 / D_MODEL, bias=EPSC[:, 0:1]).then_inc(sem("norm_log"), 1)
                act.wait_ge(sem("norm_log"), e + 1)
                fn(dst[:], dst[:], ACT.Exp, scale=-0.5).then_inc(sem(name), 1)

            def gates(t, l):
                if t == 14:
                    act.wait_ge(sem("gate_in"), 16 * 4 * (l + 1))
                    fn(GP[:, 1:2], GP[:, 1:2], ACT.Exp).then_inc(gate("rate", 0)[0], 1)
                if t == 17:
                    act.wait_ge(*gate("biased", l))
                    fn(GE[0:64], ZG[0:64], ACT.Exp, scale=2.0 / SOFTCAP).then_inc(gate("tanh_exp", 0)[0], 1)
                    fn(GE[64:96], ZG[64:96], ACT.Copy, scale=0.0, bias=1.0).then_inc(gate("idle_rows", 0)[0], 1)
                    fn(GE[96:128], ZG[96:128], ACT.Exp, scale=-1.0).then_inc(gate("beta_exp", 0)[0], 1)
                if t == 19:
                    act.wait_ge(*gate("abs", l))
                    fn(GE[:], GE[:], ACT.Exp, scale=-1.0).then_inc(gate("sp_exp", 0)[0], 1)
                    act.wait_ge(*gate("rest", l))
                    fn(GT[:], GT[:], ACT.Ln).then_inc(gate("log", 0)[0], 1)
                if t == 24:
                    act.wait_ge(*gate("sums", l))
                    fn(GT[64:96], GU[64:96], ACT.Exp).then_inc(gate("gamma", 0)[0], 1)
                    act.wait_ge(*gate("kd_log", l))
                    fn(ROWB[64:96], ROWB[64:96], ACT.Exp, scale=-1.0).then_inc(gate("kd_exp", 0)[0], 1)
                if t == 27:
                    act.wait_ge(*gate("m", l))
                    fn(EM[:], MC, ACT.Exp, scale=-1.0).then_inc(gate("em", 0)[0], 1)
                    act.wait_ge(*gate("wl_log", l))
                    fn(ROWA[32:32 + H_A], ROWB[0:H_A], ACT.Exp).then_inc(gate("wl_exp", 0)[0], 1)
                    act.wait_ge(*gate("inter_log", l))
                    fn(IR[:, SEQ:T], IR[:, SEQ:T], ACT.Exp).then_inc(gate("inter", 0)[0], 1)

            def store_prompt_state(n):
                act.wait_ge(sem("state_kept"), n + 1)
                act.dma_start(d["sout"][bass.ds(n, 1), :, 0:HD].rearrange("a p e -> p (a e)"), SOUT[:]).then_inc(sem("prompt_out"), 16)

            def gate_exp(n, par):
                act.wait_ge(sem("z_ready"), 4 * n + 4)
                fn(GATE[:], Z[par][:, 3], ACT.Exp, scale=-1.0).then_inc(sem("gate_exp"), 1)

            def gate_log(n):
                act.wait_ge(sem("gate_sum"), n + 1)
                fn(LG[:], GATE[:], ACT.Ln).then_inc(sem("gate_log"), 1)

            def head_scale(n):
                act.wait_ge(sem("head_sums"), n + 1)
                fn(SQH[:], PD[:, 0:T], ACT.Ln, scale=1.0 / HD, bias=EPSC[:, 0:1]).then_inc(sem("head_log"), 1)
                act.wait_ge(sem("scale_log"), n + 1)
                fn(GATE[:], LG[:], ACT.Exp, scale=-1.0).then_inc(sem("head_scale"), 1)

            def linear_head(step, kind, x):
                n, nk, hk, par, pair = x
                mls = kind == "mls"
                if step == 0:
                    gate_exp(n, par)
                if step == 1:
                    gate_log(n)
                    if mls:
                        act.wait_ge(sem("mls_logw"), 4 * (nk + 1))
                        fn(LW[:, 0:384], LW[:, 0:384], ACT.Exp).then_inc(sem("mls_w"), 1)
                        fn(LW[0:NS, 384:416], LW[0:NS, 384:416], ACT.Exp).then_inc(sem("mls_w"), 1)
                if step == 2:
                    act.wait_ge(sem("kv_turned"), n + 1)
                    cols = CUR[:, :, 1] if mls else AUX[par][:, AUX_TAP:AUX_TAP + 3]
                    if mls:
                        act.wait_ge(sem("mls_cur"), 2 * (nk + 1))
                    else:
                        act.wait_ge(sem(f"aux_in{par}"), aux_count(kind, x))
                    fn(U_[:, 0:2].rearrange("p a b -> p (a b)"), PB[:, 0:SEQ]).then_inc(sem(f"{kind}_kept"), 1)
                    for j, (a, b, m) in enumerate(TILES):
                        fn(KW[0:m, j], PA[0:m, j * HD:(j + 1) * HD], scale=cols[0:m, j:j + 1]).then_inc(sem(f"{kind}_kept"), 1)
                    fn(U_[0:NS, 2], PB[0:NS, SEQ:SEQ + HD]).then_inc(sem(f"{kind}_kept"), 1)
                    act.wait_ge(sem(f"{kind}_kept"), 5 * (nk + 1))
                    act.sem_inc(sem("sample_values"), 1)
                if step == 3:
                    act.wait_ge(sem("prompt_state"), n + 1)
                    act.wait_ge(sem("prompt_out"), 16 * (n + 1))
                    fn(SOUT[:], PD[:, 0:HD]).then_inc(sem("state_kept"), 1)
                if step == 4 and mls:
                    act.wait_ge(sem("mls_nout"), 3 * (nk + 1))
                    act.dma_start(d["nout"][bass.ds(nk, 1)].rearrange("a p b -> p (a b)"), NOUT[:]).then_inc(sem("norm_out"), 16)
                if step == 5:
                    store_prompt_state(n)
                    act.wait_ge(sem(f"{kind}_head"), nk + 1)
                    fn(SQH[:], HHD[:], ACT.Square).then_inc(sem("head_squares"), 1)
                if step == 8:
                    head_scale(n)

            def gdn_front(t, x):
                n, nk, hk, par, pair = x
                z = Z[par]
                for c in range(3):
                    first = CONV_SLOTS[c]
                    if t == first:
                        act.wait_ge(sem("z_ready"), 4 * n + c + 1)
                        if c == 0:
                            act.wait_ge(sem(f"aux_in{par}"), aux_count("gdn", x))
                        cs = CB[:, c, CB_P:CB_N].rearrange("p (b w) -> p b w", b=NB)
                        st = AUX[par][:, AUX_STATE:AUX_STATE + CONVS].rearrange("p (c b w) -> p c b w", c=3, b=NB)
                        fn(CB[:, c, CONVW - 1:CB_P], z[:, c, 0:SEQ]).then_inc(sem("gdn_conv_in"), 1)
                        fn(cs[:, :, CONVW - 1:], z[:, c, SEQ:T].rearrange("p (b t) -> p b t", b=NB)).then_inc(sem("gdn_conv_in"), 1)
                        fn(cs[:, :, 0:CONVW - 1], st[:, c]).then_inc(sem("gdn_conv_in"), 1)
                    if t == first + EXP_AFTER[c]:
                        act.wait_ge(sem("gdn_taps"), 12 * nk + 4 * c + 4)
                        fn(EE[:, c], ACC[:, c], ACT.Exp, scale=-1.0).then_inc(sem("gdn_silu_exp"), 1)
                    if t == first + LOG_AFTER[c]:
                        act.wait_ge(sem("gdn_silu_sum"), 3 * nk + c + 1)
                        fn(EE[:, c], EE[:, c], ACT.Ln).then_inc(sem("gdn_silu_log"), 1)
                        act.wait_ge(sem("gdn_silu_log"), 3 * nk + c + 1)
                        fn(EE[:, c], EE[:, c], ACT.Exp, scale=-1.0).then_inc(sem("gdn_sigmoid"), 1)
                    if t == first + 7 and c < 2:
                        act.wait_ge(sem("gdn_qkv"), 6 * nk + 2 * c + 2)
                        fn(EE[:, c, 0:T], z[:, c], ACT.Square).then_inc(sem("gdn_squares"), 1)
                for c, slot in ((0, 21), (1, 25)):
                    if t == slot:
                        act.wait_ge(sem("gdn_sums"), 2 * nk + c + 1)
                        fn(EE[:, c, 0:T], PE_[:, 0:T], ACT.Ln, bias=EPSC[:, 0:1]).then_inc(sem("gdn_l2_log"), 1)
                        act.wait_ge(sem("gdn_l2_log"), 2 * nk + c + 1)
                        fn(EE[:, c, 0:T], EE[:, c, 0:T], ACT.Exp, scale=-0.5).then_inc(sem("gdn_l2"), 1)
                if t == 30:
                    act.wait_ge(sem("cnew_out"), 16 * (nk + 1))
                    act.wait_ge(sem("gdn_conv_in"), 9 * (nk + 1))
                    fn(CNEW[:, :, 0:3], CB[:, :, SEQ:SEQ + 3]).then_inc(sem("cnew_ready"), 1)
                    cs = CB[:, :, CB_P:CB_N].rearrange("p c (b w) -> p c b w", b=NB)
                    for c in range(3):
                        fn(CNEW[:, c, 3:].rearrange("p (b w) -> p b w", b=NB), cs[:, c, :, DS:]).then_inc(sem("cnew_ready"), 1)
                if t == 31:
                    act.wait_ge(sem("cnew_ready"), 4 * (nk + 1))
                    act.dma_start(d["cnew"][bass.ds(nk, 1)].rearrange("a p w -> p (a w)"),
                                  CNEW[:].rearrange("p c w -> p (c w)")).then_inc(sem("cnew_out"), 16)

            def gdn_head(t, x):
                n, nk, hk, par, pair = x
                if t == 1:
                    act.wait_ge(sem(f"bc_in{par}"), aux_count("gdn", x))
                    act.wait_ge(sem("gdn_dx"), 3 * (nk + 1))
                    fn(DX, DX, ACT.Exp, scale=-1.0).then_inc(sem("gdn_decay"), 1)
                    act.wait_ge(sem("gdn_dx2"), 3 * (nk + 1))
                    fn(SC[:, 0:T], SC[:, 0:T], ACT.Exp).then_inc(sem("gdn_decay2"), 1)
                if t == 5:
                    act.wait_ge(sem("kv_turned"), n + 1)
                    act.wait_ge(sem("gdn_cur"), 3 * (nk + 1))
                for j, (a, b, m) in enumerate(TILES):
                    if t == 5 + j:
                        fn(KW[0:m, j], PA[0:m, j * HD:(j + 1) * HD], scale=CUR[0:m, j, 2:3]).then_inc(sem("gdn_kept"), 1)
                        fn(V_[0:m, j], PB[0:m, j * HD:(j + 1) * HD], scale=CUR[0:m, j, 1:2]).then_inc(sem("gdn_kept"), 1)
                if t == 6:
                    gate_exp(n, par)
                if t == 8:
                    gate_log(n)
                if t == 19:
                    act.wait_ge(sem("gdn_u0"), nk + 1)
                    fn(U_[:, 0], PA[:, 0:HD]).then_inc(sem("gdn_u0_kept"), 1)
                    act.wait_ge(sem("state_read"), n + 1)
                    fn(SMALL[:, 0], PF[:, T:T + NS]).then_inc(sem("gdn_ks_kept"), 1)
                if t == 20:
                    act.wait_ge(sem("gdn_s1"), nk + 1)
                    fn(S1[:], PB[:, 0:HD]).then_inc(sem("gdn_s1_kept"), 1)
                if t == 22:
                    act.wait_ge(sem("gdn_us"), nk + 1)
                    fn(U_[0:NS, 2], PC[0:NS, HD:2 * HD], scale=-1.0).then_inc(sem("sample_values"), 1)
                if t == 24:
                    act.wait_ge(sem("gdn_u1"), nk + 1)
                    fn(U_[:, 1], PA[:, HD:2 * HD], scale=-1.0).then_inc(sem("gdn_u1_kept"), 1)
                if t == 27:
                    store_prompt_state(n)
                    act.wait_ge(sem("gdn_head"), nk + 1)
                    fn(SQH[:], HHD[:], ACT.Square).then_inc(sem("head_squares"), 1)
                if t == 29:
                    head_scale(n)

            def mixer(t, kind, l, x, last=False):
                if kind == "gdn":
                    gdn_head(t, x)
                elif kind in ("ret", "mls"):
                    for step, slot in (LAST_SLOTS if last else LINEAR_SLOTS).items():
                        if t == slot:
                            linear_head(step, kind, x)
                elif kind == "first":
                    gates(t, l)

            def quad(Q, kind, l, x, front=None, last_head=None):
                for t in range(SLOTS):
                    mixer(t, kind, l, x)
                    if last_head:
                        mixer(t, "mls", l, last_head, last=True)
                    if front:
                        gdn_front(t, front)
                    s, c = divmod(t, 8)
                    if kind in ("out", "down_last") and c == 7:
                        output_squares(t, kind, l, x)
                    if kind in ("up", "up_first") and c == 7:
                        act.wait_ge(sem("up_relu"), up_units(l, x, s) + 1)
                        fn(UPT[s % 2], UPE[s % 2], ACT.Square).then_inc(sem("up_square"), 1)
                    if t % 2:
                        hi_part(Q, (t + 1) // 2 + 4)

            def after_out(l):
                norm_scale(4 * l + 1, RS, "rs_ready")
                prenorm(l, 2, NG[:, 1])

            def after_mlp(l):
                norm_scale(4 * l + 3, RS, "rs_ready")

            act.wait_ge(sem("ones_set"), 1)
            for p in range(5):
                hi_part(0, p)
            walk(act, lambda l: prenorm(l, 0, NG0), quad, after_out, after_mlp)
            act.wait_ge(sem("cnew_out"), 16 * (DEPTH * H_C + 1))
            act.wait_ge(sem("norm_out"), 16 * (DEPTH * H_A + 1))
            act.wait_ge(sem("prompt_out"), 16 * (DEPTH * HEADS + 1))

        @block.vector
        def _(dve):
            tt, ts, stt = nc.vector.tensor_tensor, nc.vector.tensor_scalar, nc.vector.scalar_tensor_tensor

            def lo_part(Q, p):
                s, c = divmod(p, 4)
                if c == 0:
                    dve.wait_ge(sem("unit_done"), 4 * Q + s + 1)
                dve.wait_ge(sem("hi_ready"), 16 * Q + p + 1)
                k = slice(4 * c, 4 * c + 4)
                tt(WL[s % 2][:, k], RAW[c][:], WH[s % 2][:, k].bitcast(F32), ALU.subtract).then_inc(sem("lo_ready"), 1)

            def prenorm_lo(l, which, gain, chunks=range(NC_)):
                for c in chunks:
                    dve.wait_ge(sem("hh_ready"), (2 * l + which) * NC_ + c + 1)
                    stt(HL[:, c], X[:, c], gain[:, c:c + 1], HH[:, c].bitcast(F32), ALU.mult, ALU.subtract)\
                        .then_inc(sem("hl_ready"), 1)

            def update_x(l, which, gain, g):
                e = 2 * l + which
                if g == 0:
                    dve.wait_ge(sem("rs_ready"), e + 1)
                for c in (2 * g, 2 * g + 1):
                    stt(Y[:, c], Y[:, c], gain[:, c:c + 1], RS[:], ALU.mult, ALU.mult).then_inc(sem("y_scaled"), 1)
                dve.wait_ge(sem("y_scaled"), NC_ * e + 2 * g + 2)
                k = slice(2 * g, 2 * g + 2)
                tt(X[:, k], X[:, k], Y[:, k], ALU.add).then_inc(sem("x_updated"), 1)

            def gates(t, l):
                if t == 0:
                    dve.wait_ge(sem("constants_in"), 16 * len(con))
                    dve.wait_ge(sem("gate_in"), 16 * 4 * (l + 1))
                    dve.wait_ge(sem("first_gain_in"), 16 * (l + 1))
                    tt(GWf, GWf, NG0[:].unsqueeze(2).to_broadcast([128, NC_, HD]), ALU.mult).then_inc(gate("weights", 0)[0], 1)
                if t == 15:
                    dve.wait_ge(sem("s_ready"), 2 * l + 1)
                    dve.wait_ge(*gate("proj", l))
                    tt(ZG, PD[:, 0:T], S[:], ALU.mult).then_inc(gate("z", 0)[0], 1)
                    dve.wait_ge(*gate("z", l))
                    ts(ZG, ZG, GP[:, 0:1], None, ALU.add).then_inc(gate("biased", 0)[0], 1)
                if t == 17:
                    dve.wait_ge(*gate("tanh_exp", l))
                    dve.wait_ge(*gate("beta_exp", l))
                    for r in (slice(0, 64), slice(96, 128)):
                        ts(GE[r], GE[r], 1.0, None, ALU.add).then_inc(gate("rec_sum", 0)[0], 1)
                    dve.wait_ge(*gate("rec_sum", l))
                    nc.vector.reciprocal(GE[:], GE[:]).then_inc(gate("rec", 0)[0], 1)
                    dve.wait_ge(*gate("rec", l))
                    ts(GU[0:64], GE[0:64], -2.0 * SOFTCAP, SOFTCAP, ALU.mult, ALU.add).then_inc(gate("capped", 0)[0], 1)
                    ts(ROWA[96:128], GE[96:128], 1.0, None, ALU.mult).then_inc(gate("beta", 0)[0], 1)
                    dve.wait_ge(*gate("capped", l))
                    ts(ZG[0:64], GU[0:64], -1.0, None, ALU.mult).then_inc(gate("y", 0)[0], 1)
                    dve.wait_ge(*gate("y", l))
                    stt(GE, ZG, -1.0, ZG, ALU.mult, ALU.max).then_inc(gate("abs", 0)[0], 1)
                if t == 19:
                    dve.wait_ge(*gate("sp_exp", l))
                    ts(GT, GE, 1.0, None, ALU.add).then_inc(gate("u", 0)[0], 1)
                    dve.wait_ge(*gate("u", l))
                    stt(SQH[:], GT, -1.0, GE, ALU.add, ALU.subtract).then_inc(gate("rest", 0)[0], 1)
                    dve.wait_ge(*gate("log", l))
                    dve.wait_ge(*gate("rest", l))
                    tt(GT, GT, SQH[:], ALU.subtract).then_inc(gate("log1p", 0)[0], 1)
                    dve.wait_ge(*gate("log1p", l))
                    stt(GT, ZG, 0.0, GT, ALU.max, ALU.add).then_inc(gate("softplus", 0)[0], 1)
                    dve.wait_ge(*gate("softplus", l))
                    dve.wait_ge(*gate("rate", l))
                    ts(GT, GT, GP[:, 1:2], -1.0, ALU.mult, ALU.mult).then_inc(gate("decay", 0)[0], 1)
                if t == 21:
                    ts(EXTI[:, 1:EXT_P], GU[0:H_A, 0:SEQ], 1.0, None, ALU.mult).then_inc(gate("ext", 0)[0], 1)
                    ei = EXTI[:, EXT_P:EXT].rearrange("p (b t) -> p b t", b=NB)
                    ef = EXTF[:, EXT_P:EXT].rearrange("p (b t) -> p b t", b=NB)
                    ts(ei[:, :, 1:], sview(GU[0:H_A]), 1.0, None, ALU.mult).then_inc(gate("ext", 0)[0], 1)
                    ts(ei[:, :, 0:1], MI[:].unsqueeze(2), 1.0, None, ALU.mult).then_inc(gate("ext", 0)[0], 1)
                    nc.vector.memset(EXTI[:, 0:1], 0.0).then_inc(gate("ext", 0)[0], 1)
                    nc.vector.memset(EXTF, BIG).then_inc(gate("ext_f", 0)[0], 1)
                    dve.wait_ge(*gate("decay", l))
                    dve.wait_ge(*gate("ext_f", l))
                    ts(EXTF[:, 1:EXT_P], GT[32:32 + H_A, 0:SEQ], 1.0, None, ALU.mult).then_inc(gate("ext", 0)[0], 1)
                    ts(ef[:, :, 1:], sview(GT[32:32 + H_A]), 1.0, None, ALU.mult).then_inc(gate("ext", 0)[0], 1)
                    dve.wait_ge(*gate("ext", l))
                    nc.vector.tensor_tensor_scan(SQH[:], RESETS, GT, 0.0, ALU.mult, ALU.add).then_inc(gate("scan", 0)[0], 1)
                    nc.vector.tensor_tensor_scan(EXTM, EXTF, EXTI, 0.0, ALU.add, ALU.max).then_inc(gate("scan", 0)[0], 1)
                    dve.wait_ge(*gate("scan", l))
                    ts(LG[0:H_A], GU[0:H_A], 1.0, None, ALU.mult).then_inc(gate("i", 0)[0], 1)
                    ts(F0, SQH[32:32 + H_A], 1.0, None, ALU.mult).then_inc(gate("f", 0)[0], 1)
                    ts(MC[:, 0:SEQ], EXTM[:, 1:EXT_P], 1.0, None, ALU.mult).then_inc(gate("m", 0)[0], 1)
                    em = EXTM[:, EXT_P:EXT].rearrange("p (b t) -> p b t", b=NB)
                    ts(sview(MC), em[:, :, 1:], 1.0, None, ALU.mult).then_inc(gate("m", 0)[0], 1)
                    dve.wait_ge(*gate("i", l))
                    ts(GU[64:96], SQH[64:96], 1.0, None, ALU.mult).then_inc(gate("sums", 0)[0], 1)
                    ts(MOUT[:, 0:1], EXTM[:, SEQ:SEQ + 1], 1.0, None, ALU.mult).then_inc(gate("mout", 0)[0], 1)
                    ts(MOUT[:, 1:].unsqueeze(2), em[:, :, DS:DS + 1], 1.0, None, ALU.mult).then_inc(gate("mout", 0)[0], 1)
                if t == 24:
                    ts(ROWA[64:96], SQH[64:96], 1.0, None, ALU.mult).then_inc(gate("rows", 0)[0], 1)
                    dve.wait_ge(*gate("sums", l))
                    for a, b in ((0, HD), (HD, SEQ)):
                        ts(ROWB[64:96, a:b], GU[64:96, a:b], GU[64:96, b - 1:b], None, ALU.subtract).then_inc(gate("kd_log", 0)[0], 1)
                    gu = sview(GU[64:96])
                    tt(sview(ROWB[64:96]), gu, gu[:, :, DS - 1:DS].to_broadcast([32, NB, DS]), ALU.subtract).then_inc(gate("kd_log", 0)[0], 1)
                    dve.wait_ge(*gate("m", l))
                    dve.wait_ge(*gate("f", l))
                    tt(AR[:], F0, MC, ALU.subtract).then_inc(gate("a", 0)[0], 1)
                    tt(ROWA[0:H_A], LG[0:H_A], F0, ALU.subtract).then_inc(gate("b", 0)[0], 1)
                    dve.wait_ge(*gate("a", l))
                    dve.wait_ge(*gate("b", l))
                    ts(ROWB[0:H_A, 0:SEQ], ROWA[0:H_A, 0:SEQ], AR[:, SEQ - 1:SEQ], None, ALU.add).then_inc(gate("wl_log", 0)[0], 1)
                    ar = sview(AR)
                    tt(sview(ROWB[0:H_A]), sview(ROWA[0:H_A]), ar[:, :, DS - 1:DS].to_broadcast([H_A, NB, DS]), ALU.add)\
                        .then_inc(gate("wl_log", 0)[0], 1)
                    tt(sview(IR), ar, MI[:].unsqueeze(2).to_broadcast([H_A, NB, DS]), ALU.add).then_inc(gate("inter_log", 0)[0], 1)
                if t == 29:
                    dve.wait_ge(*gate("wl_exp", l))
                    ts(ROWA[32:32 + H_A], ROWA[32:32 + H_A], SCALE, None, ALU.mult).then_inc(gate("wl", 0)[0], 1)
                if t == 31:
                    dve.wait_ge(*gate("turned", l))
                    for dst, src in ((COLA, PE_), (COLB, PF)):
                        nc.vector.tensor_copy(dst[:, 0:2].rearrange("p a b -> p (a b)"), src[:, 0:SEQ]).then_inc(gate("cols", 0)[0], 1)
                        nc.vector.tensor_copy(dst[0:NS, 2], src[0:NS, SEQ:SEQ + HD]).then_inc(gate("cols", 0)[0], 1)

            def cap_gate(n):
                dve.wait_ge(sem("gate_exp"), n + 1)
                ts(GATE[:], GATE[:], CAP, 1.0, ALU.min, ALU.add).then_inc(sem("gate_sum"), 1)

            def finish(n, par, silu):
                dve.wait_ge(sem("head_log"), n + 1)
                dve.wait_ge(sem("gate_log"), n + 1)
                stt(LG[:], SQH[:], 0.5, LG[:], ALU.mult, ALU.add).then_inc(sem("scale_log"), 1)
                dve.wait_ge(sem("head_scale"), n + 1)
                stt(YY[:], HHD[:], AUX[par][:, AUX_GAIN:AUX_GAIN + 1], GATE[:], ALU.mult, ALU.mult).then_inc(sem("y_head"), 1)
                dve.wait_ge(sem("y_head"), n + 1)
                y = YY
                if silu:
                    tt(HHD[:], YY[:], Z[par][:, 3], ALU.mult).then_inc(sem("y_gated"), 1)
                    y = HHD
                return y

            def store_u(n, l, c, y):
                ts(UH[:, c].rearrange("p a t -> p (a t)"), y[:], 1.0, None, ALU.mult).then_inc(sem("uh_head"), 1)
                dve.wait_ge(sem("uh_head"), n + 1)
                tt(UL[:, c].rearrange("p a t -> p (a t)"), y[:], UH[:, c].rearrange("p a t -> p (a t)").bitcast(F32), ALU.subtract)\
                    .then_inc(sem("ul_ready"), 1)
                dve.wait_ge(sem("ul_ready"), l * (NC_ * MLP_Q) + n + 1)
                dve.sem_inc(sem("head_done"), 1)

            def add_state(n):
                dve.wait_ge(sem("sample_state"), n + 1)
                dve.wait_ge(sem("state_decayed"), n + 1)
                dve.wait_ge(sem("state_kept"), n + 1)
                tt(CDEC.rearrange("p b e -> p (b e)"), CDEC.rearrange("p b e -> p (b e)"),
                   PAB[:].rearrange("p a b -> p (a b)"), ALU.add).then_inc(sem("state_ready"), 1)

            def chunk_of(kind, hk):
                base = {"gdn": 0, "ret": H_C, "mls": H_C + H_B}[kind]
                return bass.ds(base + hk, 1)

            def linear_head(step, kind, l, x):
                n, nk, hk, par, pair = x
                mls = kind == "mls"
                z, bc, aux = Z[par], BC[par], AUX[par]
                if step == 0:
                    cap_gate(n)
                    dve.wait_ge(sem(f"aux_in{par}"), aux_count(kind, x))
                    if mls:
                        for j, r in ((0, 0), (1, 32)):
                            if j == 0:
                                dve.wait_ge(*gate("cols", l))
                            ts(CUR[:, :, j:j + 1], COLA[:, :, bass.ds(hk + r, 1)], 1.0, None, ALU.mult).then_inc(sem("mls_cur"), 1)
                if step == 1 and not mls:
                    tt(ACC[:, 0:2, 0:T], z[:, 0:2], con["c_cos"][:].unsqueeze(1).to_broadcast([128, 2, T]), ALU.mult)\
                        .then_inc(sem("ret_qk"), 1)
                    dve.wait_ge(sem("ret_rotated"), nk + 1)
                    tt(EE[:, 0:2, 0:T], PCD[:, :, 0:T], con["c_sin"][:].unsqueeze(1).to_broadcast([128, 2, T]), ALU.mult)\
                        .then_inc(sem("ret_qk"), 1)
                    dve.wait_ge(sem("ret_qk"), 3 * nk + 2)
                    tt(QK2, ACC[:, 0:2, 0:T], EE[:, 0:2, 0:T], ALU.add).then_inc(sem("ret_qk"), 1)
                if step == 1 and mls:
                    dve.wait_ge(sem("mls_cur"), 2 * (nk + 1))
                    dve.wait_ge(sem(f"bc_in{par}"), aux_count(kind, x))
                    never = con["c_never"]
                    stt(LW[:, 0:HD], bc[:, 0:HD], CUR[:, 0, 0:1], never[:], ALU.add, ALU.add).then_inc(sem("mls_logw"), 1)
                    ts(LW[:, HD:SEQ], bc[:, HD:SEQ], CUR[:, 0, 0:1], None, ALU.add).then_inc(sem("mls_logw"), 1)
                    stt(LW[:, SEQ:384], bc[:, HD:SEQ], CUR[:, 1, 0:1], never[:], ALU.add, ALU.add).then_inc(sem("mls_logw"), 1)
                    stt(LW[0:NS, 384:416], bc[0:NS, SEQ:T], CUR[0:NS, 2, 0:1], con["c_never_s"][0:NS], ALU.add, ALU.add)\
                        .then_inc(sem("mls_logw"), 1)
                if step == 2:
                    q = z[:, 0] if mls else QK2[:, 0]
                    if not mls:
                        dve.wait_ge(sem("ret_qk"), 3 * (nk + 1))
                        dve.wait_ge(sem(f"bc_in{par}"), aux_count(kind, x))
                    tt(SMALL[:, 0], q[:, SEQ:T], bc[:, 2 * T:], ALU.mult).then_inc(sem(f"{kind}_qs"), 1)
                    dve.wait_ge(sem("scores"), n + 1)
                    if mls:
                        dve.wait_ge(sem("mls_w"), 2 * (nk + 1))
                        stt(SC[:, 0:384], PE_[:, 0:384], SCALE, LW[:, 0:384], ALU.mult, ALU.mult).then_inc(sem("mls_probs"), 1)
                        stt(SC[0:NS, 384:416], PE_[0:NS, 384:416], SCALE, LW[0:NS, 384:416], ALU.mult, ALU.mult)\
                            .then_inc(sem("mls_probs"), 1)
                        dve.wait_ge(sem("mls_qs"), nk + 1)
                        nin = aux[:, AUX_STATE:AUX_STATE + NB].unsqueeze(2).to_broadcast([128, NB, DS])
                        tt(SMALL[:, 1].rearrange("p (b t) -> p b t", b=NB), SMALL[:, 0].rearrange("p (b t) -> p b t", b=NB),
                           nin, ALU.mult).then_inc(sem("mls_qn"), 1)
                    else:
                        dm = aux[:, AUX_STATE:AUX_STATE + T]
                        stt(SC[:, 0:SEQ], PE_[:, 0:SEQ], SCALE, dm[:, 0:SEQ], ALU.mult, ALU.mult).then_inc(sem("ret_probs"), 1)
                        stt(SC[:, SEQ:384], PE_[:, SEQ:384], SCALE, dm[:, 0:HD], ALU.mult, ALU.mult).then_inc(sem("ret_probs"), 1)
                        stt(SC[0:NS, 384:416], PE_[0:NS, 384:416], SCALE, dm[0:NS, SEQ:T], ALU.mult, ALU.mult)\
                            .then_inc(sem("ret_probs"), 1)
                if step == 3:
                    dve.wait_ge(sem(f"{kind}_out"), nk + 1)
                    if mls:
                        stt(YY[:], PC[:, 0:T], -1.0, bc[:, T:2 * T], ALU.mult, ALU.max).then_inc(sem("mls_den"), 1)
                        dve.wait_ge(sem("mls_den"), 3 * nk + 1)
                        tt(YY[:], PC[:, 0:T], YY[:], ALU.max).then_inc(sem("mls_den"), 1)
                        dve.wait_ge(sem("mls_den"), 3 * nk + 2)
                        nc.vector.reciprocal(YY[:], YY[:]).then_inc(sem("mls_den"), 1)
                        dve.wait_ge(sem("mls_den"), 3 * nk + 3)
                        tt(HHD[:], PF[:, 0:T], YY[:], ALU.mult).then_inc(sem("mls_head"), 1)
                        dve.wait_ge(sem("prompt_state"), n + 1)
                        dve.wait_ge(sem("norm_out"), 16 * (nk + 1))
                        tt(NOUT[:, 1:], aux[:, AUX_STATE:AUX_STATE + NB], bc[:, 2 * T + DS - 1:BCW:DS], ALU.mult)\
                            .then_inc(sem("mls_nout"), 1)
                        dve.wait_ge(sem("mls_nout"), 3 * nk + 1)
                        dve.wait_ge(sem("state_kept"), n + 1)
                        tt(NOUT[:, 1:], NOUT[:, 1:], PD[:, HD + 1:HD + 1 + NB], ALU.add).then_inc(sem("mls_nout"), 1)
                        nc.vector.tensor_copy(NOUT[:, 0:1], PD[:, HD:HD + 1]).then_inc(sem("mls_nout"), 1)
                    else:
                        nc.vector.tensor_copy(YY[:], PF[:, 0:T]).then_inc(sem("ret_kept_out"), 1)
                if step == 4 and not mls:
                    dve.wait_ge(sem("ret_centered"), nk + 1)
                    nc.vector.tensor_copy(HHD[:], PC[:, 0:T]).then_inc(sem("ret_head"), 1)
                if step == 8:
                    y = finish(n, par, not mls)
                    if not mls:
                        dve.wait_ge(sem("y_gated"), silu_count(l, kind, hk))
                    store_u(n, l, chunk_of(kind, hk), y)
                if step == 10:
                    add_state(n)

            def silu_count(l, kind, hk):
                return l * (H_C + H_B) + (H_C if kind == "ret" else 0) + hk + 1

            def gdn_head(t, l, x):
                n, nk, hk, par, pair = x
                bc = BC[par]
                if t == 7:
                    cap_gate(n)
                if t == 0:
                    dve.wait_ge(*gate("cols", l))
                    for j, (src, r) in enumerate(((COLA, 64), (COLA, 96), (COLB, 64))):
                        ts(CUR[:, :, j:j + 1], src[:, :, bass.ds(hk + r, 1)], 1.0, None, ALU.mult).then_inc(sem("gdn_cur"), 1)
                    dve.wait_ge(sem(f"bc_in{par}"), aux_count("gdn", x))
                    dve.wait_ge(sem("gdn_cur"), 3 * (nk + 1))
                    for j, (a, b, m) in enumerate(TILES):
                        ts(DX[:, a:b], bc[:, a:b], CUR[:, j, 0:1], 0.0, ALU.subtract, ALU.max).then_inc(sem("gdn_dx"), 1)
                    for j, (a, b, m) in enumerate(TILES):
                        ts(SC[:, a:b], bc[:, a:b], CUR[:, j, 0:1], 0.0, ALU.subtract, ALU.min).then_inc(sem("gdn_dx2"), 1)
                if t == 3:
                    dve.wait_ge(sem("gdn_kk"), nk + 1)
                    dve.wait_ge(sem("gdn_decay"), nk + 1)
                    for j, (a, b, m) in enumerate(TILES):
                        stt(AM[0:m, a:b], PC[0:m, a:b], CUR[0:m, j, 1:2], DX[0:m, a:b], ALU.mult, ALU.mult).then_inc(sem("gdn_A"), 1)
                    dve.wait_ge(sem("scores"), n + 1)
                    dve.wait_ge(sem("gdn_decay2"), nk + 1)
                    stt(SC[:, 0:SEQ], PF[:, 0:SEQ], SCALE, SC[:, 0:SEQ], ALU.mult, ALU.mult).then_inc(sem("gdn_scores"), 1)
                    stt(SC[0:NS, SEQ:T], PF[0:NS, SEQ:T], SCALE, SC[0:NS, SEQ:T], ALU.mult, ALU.mult).then_inc(sem("gdn_scores"), 1)
                if t == 18:
                    stt(QKG[:, 0], QK2[:, 0], SCALE, bc[:, T:2 * T], ALU.mult, ALU.mult).then_inc(sem("gdn_qkg"), 1)
                    tt(QKG[:, 1], QK2[:, 1], bc[:, T:2 * T], ALU.mult).then_inc(sem("gdn_qkg"), 1)
                if t == 19:
                    dve.wait_ge(sem("gdn_scores"), 2 * (nk + 1))
                    sc = SC[:, 0:SEQ].rearrange("p (a b) -> p a b", a=2)
                    tt(sc, sc, con["c_causal"][:].unsqueeze(1).to_broadcast([128, 2, HD]), ALU.mult).then_inc(sem("gdn_probs"), 1)
                    tt(SC[0:NS, SEQ:T], SC[0:NS, SEQ:T], con["c_causal_s"][0:NS], ALU.mult).then_inc(sem("gdn_probs"), 1)
                if INVERSE_SLOT <= t < INVERSE_SLOT + 2 * LEVELS:
                    lev, second = divmod(t - INVERSE_SLOT, 2)
                    mask = con["c_levels"]
                    if not second:
                        dve.wait_ge(sem("gdn_P"), LEVELS * nk + lev + 1)
                        if lev < 2:
                            tt(PM[0:NS, SEQ:T], PD[0:NS, SEQ:T], mask[0:NS, lev, 0:NS], ALU.mult).then_inc(sem("gdn_Pm_s"), 1)
                        tt(PM[:, 0:SEQ].rearrange("p (a b) -> p a b", a=2), PD[:, 0:SEQ].rearrange("p (a b) -> p a b", a=2),
                           mask[:, lev].unsqueeze(1).to_broadcast([128, 2, HD]), ALU.mult).then_inc(sem("gdn_Pm"), 1)
                    else:
                        dve.wait_ge(sem("gdn_TR"), LEVELS * nk + lev + 1)
                        pe4 = PE_[:].rearrange("p (a b) -> p a b", a=4)
                        ident = IDENT[:].unsqueeze(1)
                        if lev < 2:
                            old = IDENT[0:NS, 0:NS].unsqueeze(1).to_broadcast([NS, 2, NS]) if lev == 0 else TS[:]
                            if lev:
                                dve.wait_ge(sem("gdn_inverse_s"), 2 * nk + 1)
                            tt(TS[:], old, PC[0:NS, 0:2 * NS].rearrange("p (a b) -> p a b", a=2), ALU.subtract)\
                                .then_inc(sem("gdn_inverse_s"), 1)
                        old = ident.to_broadcast([128, 4, HD]) if lev == 0 else TR
                        if lev:
                            dve.wait_ge(sem("gdn_inverse"), LEVELS * nk + lev)
                        tt(TR[:, 1::2], old[:, 1::2], pe4[:, 1::2], ALU.subtract).then_inc(sem("gdn_inverse"), 1)
                        if lev < LEVELS - 1:
                            if lev:
                                dve.wait_ge(sem("gdn_inverse_n"), (LEVELS - 1) * nk + lev)
                            tt(TR[:, 0::2], old[:, 0::2], pe4[:, 0::2], ALU.subtract).then_inc(sem("gdn_inverse_n"), 1)
                if t == 21:
                    dve.wait_ge(sem("gdn_ks_turned"), nk + 1)
                    dve.wait_ge(sem("gdn_kept"), 6 * (nk + 1))
                    stt(RHS[0:NS, 1], PC[0:NS, 0:HD], CUR[0:NS, 2, 1:2], V_[0:NS, 2], ALU.mult, ALU.subtract).then_inc(sem("gdn_rhs_s"), 1)
                if t == 23:
                    dve.wait_ge(sem("gdn_ks"), nk + 1)
                    stt(RHS[:, 0], PB[:, HD:2 * HD], CUR[:, 1, 1:2], V_[:, 1], ALU.mult, ALU.subtract).then_inc(sem("gdn_rhs"), 1)
                if t == 26:
                    dve.wait_ge(sem("prompt_state"), n + 1)
                    dve.wait_ge(sem("gdn_s1_kept"), nk + 1)
                    dve.wait_ge(sem("prompt_out"), 16 * (n + 1))
                    stt(SOUT[:], S1[:], bc[:, T + SEQ - 1:T + SEQ], PB[:, 2 * HD:3 * HD], ALU.mult, ALU.add).then_inc(sem("state_kept"), 1)
                    dve.wait_ge(sem("gdn_out"), nk + 1)
                    nc.vector.tensor_copy(HHD[:], PF[:, 0:T]).then_inc(sem("gdn_head"), 1)
                if t == 30:
                    add_state(n)
                    y = finish(n, par, True)
                    dve.wait_ge(sem("y_gated"), silu_count(l, "gdn", hk))
                    store_u(n, l, chunk_of("gdn", hk), y)

            def gdn_front(t, x):
                n, nk, hk, par, pair = x
                aux, z = AUX[par], Z[par]
                for c in range(3):
                    first = CONV_SLOTS[c]
                    taps = TAPS_A_SLOT[c]
                    if first < t <= first + CONVW // taps:
                        if t == first + 1:
                            dve.wait_ge(sem("gdn_conv_in"), 9 * nk + 3 * c + 3)
                        for w in range(taps * (t - first - 1), taps * (t - first)):
                            tap = aux[:, AUX_TAP + 4 * c + w:AUX_TAP + 4 * c + w + 1]
                            if w == 0:
                                ts(ACC[:, c], CB[:, c, w:w + CO], tap, None, ALU.mult).then_inc(sem("gdn_taps"), 1)
                            else:
                                dve.wait_ge(sem("gdn_taps"), 12 * nk + 4 * c + w)
                                stt(ACC[:, c], CB[:, c, w:w + CO], tap, ACC[:, c], ALU.mult, ALU.add).then_inc(sem("gdn_taps"), 1)
                    if t == first + EXP_AFTER[c] + 1:
                        dve.wait_ge(sem("gdn_silu_exp"), 3 * nk + c + 1)
                        ts(EE[:, c], EE[:, c], CAP, 1.0, ALU.min, ALU.add).then_inc(sem("gdn_silu_sum"), 1)
                    if t == first + LOG_AFTER[c] + 1:
                        dve.wait_ge(sem("gdn_sigmoid"), 3 * nk + c + 1)
                        tt(z[:, c, 0:SEQ], ACC[:, c, 0:SEQ], EE[:, c, 0:SEQ], ALU.mult).then_inc(sem("gdn_qkv"), 1)
                        tt(z[:, c, SEQ:T].rearrange("p (b t) -> p b t", b=NB), samples(ACC, c), samples(EE, c), ALU.mult)\
                            .then_inc(sem("gdn_qkv"), 1)
                for c, slot in ((0, 23), (1, 27)):
                    if t == slot:
                        dve.wait_ge(sem("gdn_l2"), 2 * nk + c + 1)
                        tt(QK2[:, c], z[:, c], EE[:, c, 0:T], ALU.mult).then_inc(sem("gdn_qk"), 1)

            def samples(a, c):
                pad = CONVW - 1
                return a[:, c, CB_P - pad:CO].rearrange("p (b t) -> p b t", b=NB)[:, :, pad:]

            def evac(Q, s, kind, l, x):
                dve.wait_ge(sem("unit_done"), 4 * Q + s + 3)
                psum = PU[s % 2][:, 0:T]
                if kind in ("first", "gdn", "ret", "mls"):
                    if kind == "first" and s == 0:
                        dve.wait_ge(sem("s_ready"), 2 * l + 1)
                    par = 0 if kind == "first" else 1 - x[3]
                    i = tt(Z[par][:, s], psum, S[:], ALU.mult)
                    i.then_inc(sem("z_ready"), 1)
                    dve.wait_ge(sem("z_ready"), z_before(Q, kind, l, x) + s + 1)
                elif kind in ("up", "up_first"):
                    u = up_units(l, x, s)
                    if s == 0:
                        dve.wait_ge(sem("s_ready"), 2 * l + 2)
                    stt(UPE[s % 2], psum, 0.0, S[:], ALU.max, ALU.mult).then_inc(sem("up_relu"), 1)
                    dve.wait_ge(sem("up_relu"), u + 1)
                elif kind == "out":
                    c = bass.ds(4 * x[1] + s, 1)
                    if s == 0:
                        dve.wait_ge(sem("state_ready"), (l + 1) * HEADS + 1)
                        dve.wait_ge(sem("state_out"), 16 * HEADS * (l + 1))
                    ts(Y[:, c].rearrange("p a t -> p (a t)"), psum, 1.0, None, ALU.mult).then_inc(sem("y_ready"), 1)
                    dve.wait_ge(sem("y_ready"), l * NC_ + 4 * x[1] + s + 1)
                else:
                    c = bass.ds(4 * x[1] + s, 1)
                    yc = Y[:, c].rearrange("p a t -> p (a t)")
                    if kind == "down0":
                        ts(yc, psum, 1.0, None, ALU.mult).then_inc(sem("y_added"), 1)
                    else:
                        tt(yc, yc, psum, ALU.add).then_inc(sem("y_added"), 1)
                    dve.wait_ge(sem("y_added"), (l * MLP_Q + x[0]) * NC_ + 4 * x[1] + s + 1)
                dve.sem_inc(sem("psum_read"), 1)

            def z_before(Q, kind, l, x):
                return l * (4 * HEADS) if kind == "first" else 4 * (x[0] + 1)

            def store_up(l, x, s):
                u = up_units(l, x, s)
                dve.wait_ge(sem("up_square"), u + 1)
                c = bass.ds(4 * x[1] + s, 1)
                uh = UH[:, c].rearrange("p a t -> p (a t)")
                ts(uh, UPT[s % 2], 1.0, None, ALU.mult).then_inc(sem("uh_ready"), 1)
                dve.wait_ge(sem("uh_ready"), u + 1)
                tt(UL[:, c].rearrange("p a t -> p (a t)"), UPT[s % 2], uh.bitcast(F32), ALU.subtract).then_inc(sem("ul_ready"), 1)

            def mixer(t, kind, l, x, last=False):
                if kind == "gdn":
                    gdn_head(t, l, x)
                elif kind in ("ret", "mls"):
                    for step, slot in (LAST_SLOTS if last else LINEAR_SLOTS).items():
                        if t == slot:
                            linear_head(step, kind, l, x)
                elif kind == "first":
                    gates(t, l)

            def quad(Q, kind, l, x, front=None, last_head=None):
                for t in range(SLOTS):
                    mixer(t, kind, l, x)
                    if last_head:
                        mixer(t, "mls", l, last_head, last=True)
                    if t % 2:
                        lo_part(Q, t // 2 + 4)
                    if front:
                        gdn_front(t, front)
                    if t % 8 == 7:
                        evac(Q, t // 8, kind, l, x)
                        if kind in ("up", "up_first"):
                            store_up(l, x, t // 8)

            def after_out(l):
                for g in range(8):
                    update_x(l, 0, NG[:, 0], g)
                    if g:
                        prenorm_lo(l, 1, NG[:, 1], range(2 * g - 2, 2 * g))
                prenorm_lo(l, 1, NG[:, 1], range(14, 16))

            def after_mlp(l):
                for g in range(8):
                    update_x(l, 1, NG[:, 2], g)
                dve.wait_ge(sem("x_updated"), 8 + 16 * l + 16)
                dve.sem_inc(sem("layer_free"), 1)

            for a, v in ((ONES, 1.0), (EPSC, EPS), (ROWA, 0.0), (CB0, 0.0), (CUR, 0.0), (COLA, 0.0), (COLB, 0.0)):
                nc.vector.memset(a if a is CB0 else a[:], v).then_inc(sem("constants_set"), 1)
            dve.wait_ge(sem("constants_set"), 7)
            dve.sem_inc(sem("ones_set"), 1)
            dve.sem_inc(sem("layer_free"), 1)
            dve.sem_inc(sem("state_ready"), 1)
            dve.sem_inc(sem("head_done"), 1)
            dve.sem_inc(sem("x_updated"), 8)
            for p in range(4):
                lo_part(0, p)
            walk(dve, lambda l: prenorm_lo(l, 0, NG0), quad, after_out, after_mlp)



def kernel(**inputs):
    import concourse.bacc as _bacc
    from concourse.bass_utils import run_bass_kernel_spmd as _run

    a = {k: np.ascontiguousarray(v) for k, v in inputs.items()}
    D = DEPTH
    w_in = a["w_in"]
    cols_a = [g * H_A * HD for g in range(4)]
    base_b = 4 * H_A * HD + 2 * H_A
    cols_b = [base_b + g * H_B * HD for g in range(4)]
    base_c = base_b + 4 * H_B * HD
    cols_c = [base_c + g * H_C * HD for g in range(4)]
    heads = [(cols_c, h) for h in range(H_C)] + [(cols_b, h) for h in range(H_B)] + [(cols_a, h) for h in range(H_A)]
    rows = [H_A + H_B + h for h in range(H_C)] + [H_A + h for h in range(H_B)] + list(range(H_A))

    w = np.empty((D * QUADS * 4 + 2, 128, NC_, HD), np.float32)
    n = 0
    for l in range(D):
        for cols, h in heads:
            for g in range(4):
                c = cols[g] + h * HD
                w[n] = w_in[l, :, c:c + HD].reshape(NC_, 128, HD).transpose(1, 0, 2)
                n += 1
        w_out = a["w_out"][l].reshape(HEADS, 128, D_MODEL)[rows]
        for j in range(NC_):
            w[n] = w_out[:, :, j * HD:(j + 1) * HD].transpose(1, 0, 2)
            n += 1
        for q in range(MLP_Q):
            for j in range(NC_):
                c = (q * NC_ + j) * HD
                w[n] = a["w_up"][l, :, c:c + HD].reshape(NC_, 128, HD).transpose(1, 0, 2)
                n += 1
            for j in range(NC_):
                part = a["w_down"][l, q * D_MODEL:(q + 1) * D_MODEL, j * HD:(j + 1) * HD]
                w[n] = part.reshape(NC_, 128, HD).transpose(1, 0, 2)
                n += 1
    w[n:] = w[0:2]

    base_g = 4 * H_A * HD
    end_c = base_c + 4 * H_C * HD
    gw = np.zeros((D, 128, NC_, HD), np.float32)
    for to, frm, k in ((0, base_g, H_A), (32, base_g + H_A, H_A), (64, end_c, H_C), (96, end_c + H_C, H_C)):
        gw[..., to:to + k] = w_in[:, :, frm:frm + k].reshape(D, NC_, 128, k).transpose(0, 2, 1, 3)
    gp = np.zeros((D, 128, 2), np.float32)
    gp[:, 0:H_A, 0] = a["mlstm_gate_bias"][:, :H_A]
    gp[:, 32:32 + H_A, 0] = a["mlstm_gate_bias"][:, H_A:]
    gp[:, 64:64 + H_C, 0] = a["gdn_dt_bias"]
    gp[:, 64:64 + H_C, 1] = a["gdn_A_log"]
    ng = np.stack([a[k].reshape(D, NC_, 128).transpose(0, 2, 1)
                   for k in ("norm_mix_post", "norm_mlp_pre", "norm_mlp_post")], 2).reshape(D, 128, 3 * NC_)
    ng0 = a["norm_mix_pre"].reshape(D, NC_, 128).transpose(0, 2, 1)
    ng0 = np.concatenate([ng0, ng0[:1]])
    consts = shape_constants()
    aux = np.zeros((D, HEADS, 128, AUXW), np.float32)
    aux[:, :H_C, :, AUX_GAIN] = a["norm_gdn"][:, None, :]
    aux[:, H_C:H_C + H_B, :, AUX_GAIN] = a["norm_ret"].reshape(D, H_B, 128)
    aux[:, H_C + H_B:, :, AUX_GAIN] = a["norm_mlstm"].reshape(D, H_A, 128)
    aux[:, :H_C, :, AUX_TAP:AUX_TAP + 12] = a["gdn_conv_w"].reshape(D, CONVW, 3, H_C, 128).transpose(0, 3, 4, 2, 1).reshape(D, H_C, 128, 12)
    aux[:, H_C:H_C + H_B, :, AUX_TAP:AUX_TAP + 3] = consts.pop("k_kdec").transpose(1, 0, 2)
    aux[:, H_C:H_C + H_B, :, AUX_STATE:] = consts.pop("k_dmat").transpose(1, 0, 2)
    aux[:, :H_C, :, AUX_STATE:AUX_STATE + CONVS] = a["state_gdn_conv"].reshape(D, NB, CONVW - 1, 3, H_C, 128).transpose(0, 4, 5, 3, 1, 2).reshape(D, H_C, 128, -1)
    aux[:, H_C + H_B:, :, AUX_STATE:AUX_STATE + NB] = a["state_mlstm_n"].transpose(0, 2, 3, 1)
    sin = np.concatenate([a[k].transpose(0, 2, 3, 1, 4) for k in ("state_gdn_S", "state_ret_S", "state_mlstm_C")], 1)
    x = np.concatenate([a["x_prompt"].reshape(SEQ, NC_, 128), a["x_sample"].reshape(NS, NC_, 128)]).transpose(2, 1, 0)

    feed = {
        "w": w, "x": x, "gw": gw, "gp": gp, "ng": ng, "ng0": ng0, "mi": a["state_mlstm_m"].transpose(0, 2, 1),
        "aux": aux.reshape(D * HEADS, 128, AUXW), "sin": sin.reshape(D * HEADS, 128, NB * HD), **consts,
    }
    outs = {
        "y": (128, NC_, T), "sout": (D * HEADS, 128, (1 + NB) * HD), "nout": (D * H_A, 128, 1 + NB),
        "mo": (D, H_A, 1 + NB), "cnew": (D * H_C, 128, 3 * (1 + NB) * (CONVW - 1)),
    }
    nc = _bacc.Bacc("TRN2", target_bir_lowering=False, num_devices=1)
    arrays, d = {}, {}
    for k, v in feed.items():
        v = np.ascontiguousarray(v)
        arrays[f"in_{k}"] = v
        d[k] = nc.dram_tensor(f"in_{k}", v.shape, F32, kind="ExternalInput").ap()
    for k, shape in outs.items():
        d[k] = nc.dram_tensor(f"out_{k}", shape, F32, kind="ExternalOutput").ap()
    d["bc"] = nc.dram_tensor("gate_rows", (D * HEADS, BCW), F32, kind="Internal").ap()
    build(nc, d)
    r = _run(nc, [arrays], core_ids=[0]).results[0]

    y = r["out_y"].transpose(2, 1, 0).reshape(T, D_MODEL)
    so = r["out_sout"].reshape(D, HEADS, 128, 1 + NB, HD).transpose(0, 3, 1, 2, 4)
    no = r["out_nout"].reshape(D, H_A, 128, 1 + NB).transpose(0, 3, 1, 2)
    mo = r["out_mo"].transpose(0, 2, 1)
    co = r["out_cnew"].reshape(D, H_C, 128, 3, 1 + NB, CONVW - 1).transpose(0, 4, 5, 3, 1, 2)
    co = co.reshape(D, 1 + NB, CONVW - 1, 3 * H_C * HD)
    res = [y[:SEQ].reshape(1, SEQ, D_MODEL), y[SEQ:].reshape(NB, DS, D_MODEL)]
    for b in (slice(0, 1), slice(1, None)):
        res += [so[:, b, H_C + H_B:], no[:, b], mo[:, b], so[:, b, H_C:H_C + H_B], so[:, b, :H_C], co[:, b]]
    return tuple(np.ascontiguousarray(v) for v in res)
```
